# Optimizing a Trainium2 kernel written in Bass

```python
import math
import jax, jax.numpy as jnp
from jax import lax
import numpy as np

D_MODEL = 1024
BATCH = 1
SEQ = 512
DEPTH = 2

ATTN_WIDTH = D_MODEL // 2
RNN_WIDTH = D_MODEL - ATTN_WIDTH
DIFF_HEAD_DIM = 64
N_DIFF_HEADS = ATTN_WIDTH // (2 * DIFF_HEAD_DIM)
V_HEAD_DIM = 2 * DIFF_HEAD_DIM
ROT_DIM = DIFF_HEAD_DIM // 4
ROPE_THETA = 500000.0
LRU_BLOCK = 64
N_LRU_BLOCKS = RNN_WIDTH // LRU_BLOCK
CONV_WIDTH = 4
LRU_C = 8.0
D_FF = 4 * D_MODEL
PLE_DIM = 256
Q_BLOCK = 128
EPS = 1e-6
IN_WIDTH = 3 * ATTN_WIDTH + 2 * RNN_WIDTH


def rms_norm(x, g):
    xf = x.astype(jnp.float32)
    y = xf * lax.rsqrt(jnp.mean(xf * xf, axis=-1, keepdims=True) + EPS)
    return (y * g.astype(jnp.float32)).astype(x.dtype)

def partial_rope(x, positions):
    half = ROT_DIM // 2
    inv_freq = ROPE_THETA ** (-jnp.arange(half, dtype=jnp.float32) * 2.0 / ROT_DIM)
    ang = positions.astype(jnp.float32)[..., None] * inv_freq
    cos = jnp.cos(ang)[:, :, None, None, :]
    sin = jnp.sin(ang)[:, :, None, None, :]
    xr = x[..., :ROT_DIM].astype(jnp.float32)
    x1, x2 = xr[..., :half], xr[..., half:]
    rot = jnp.concatenate([x1 * cos - x2 * sin, x2 * cos + x1 * sin], axis=-1)
    return jnp.concatenate([rot.astype(x.dtype), x[..., ROT_DIM:]], axis=-1)

def diff_attention(q, k, v, lam):
    B, S = q.shape[0], q.shape[1]
    nb = S // Q_BLOCK
    scale = DIFF_HEAD_DIM ** -0.5
    qb = q.reshape(B, nb, Q_BLOCK, N_DIFF_HEADS, 2, DIFF_HEAD_DIM).transpose(1, 0, 2, 3, 4, 5)
    q_idx = jnp.arange(S).reshape(nb, Q_BLOCK)
    k_idx = jnp.arange(S)

    def block(args):
        q_blk, qi = args
        s = jnp.einsum('bqhcd,bkhcd->bhcqk', q_blk, k).astype(jnp.float32) * scale
        mask = qi[:, None] >= k_idx[None, :]
        s = jnp.where(mask, s, -jnp.inf)
        pr = jax.nn.softmax(s, axis=-1)
        attn = pr[:, :, 0] - lam * pr[:, :, 1]
        return jnp.einsum('bhqk,bkhe->bqhe', attn.astype(v.dtype), v)

    out = lax.map(block, (qb, q_idx))
    return out.transpose(1, 0, 2, 3, 4).reshape(B, S, N_DIFF_HEADS, V_HEAD_DIM)

def causal_depthwise_conv(x, w, b):
    y = lax.conv_general_dilated(
        x, w[:, None, :].astype(x.dtype), window_strides=(1,),
        padding=[(CONV_WIDTH - 1, 0)],
        dimension_numbers=('NWC', 'WIO', 'NWC'),
        feature_group_count=x.shape[-1])
    return y + b

def rg_lru(x, w_a, b_a, w_x, b_x, lam_param):
    B, S, _ = x.shape
    xb = x.reshape(B, S, N_LRU_BLOCKS, LRU_BLOCK)
    r = jax.nn.sigmoid((jnp.einsum('bsgi,gij->bsgj', xb, w_a).reshape(B, S, RNN_WIDTH) + b_a).astype(jnp.float32))
    i = jax.nn.sigmoid((jnp.einsum('bsgi,gij->bsgj', xb, w_x).reshape(B, S, RNN_WIDTH) + b_x).astype(jnp.float32))
    log_a = -LRU_C * r * jax.nn.softplus(-lam_param.astype(jnp.float32))
    a = jnp.exp(log_a)
    b = jnp.sqrt(-jnp.expm1(2.0 * log_a)) * (i * x.astype(jnp.float32))

    def combine(left, right):
        a_l, b_l = left
        a_r, b_r = right
        return a_l * a_r, a_r * b_l + b_r

    _, h = lax.associative_scan(combine, (a, b), axis=1)
    return h.astype(x.dtype)

def first_inputs(seed: int = 0) -> dict:
    key = jax.random.key(seed)
    ks = jax.random.split(key, 24)
    f32 = jnp.float32
    nrm = lambda k, shape, s: jax.random.normal(k, shape, f32) * s
    gain = lambda k, shape: 1.0 + 0.05 * jax.random.normal(k, shape, f32)
    a0 = jax.random.uniform(ks[15], (DEPTH, RNN_WIDTH), f32, 0.9, 0.999)
    s0 = a0 ** (1.0 / LRU_C)
    lru_lambda = jnp.log(s0) - jnp.log1p(-s0)
    positions = jnp.broadcast_to(jnp.arange(SEQ, dtype=jnp.int32)[None, :], (BATCH, SEQ))
    return {
        'x': nrm(ks[0], (BATCH, SEQ, D_MODEL), 1.0),
        'p': nrm(ks[1], (DEPTH, BATCH, SEQ, PLE_DIM), 1.0),
        'positions': positions,
        'w_in': nrm(ks[2], (DEPTH, D_MODEL, IN_WIDTH), D_MODEL ** -0.5),
        'w_out': nrm(ks[3], (DEPTH, D_MODEL, D_MODEL), D_MODEL ** -0.5),
        'g_mix': gain(ks[4], (DEPTH, D_MODEL)),
        'g_subln': gain(ks[5], (DEPTH, V_HEAD_DIM)),
        'lam_q': nrm(ks[6], (DEPTH, 2, DIFF_HEAD_DIM), 0.1),
        'lam_k': nrm(ks[7], (DEPTH, 2, DIFF_HEAD_DIM), 0.1),
        'conv_w': nrm(ks[8], (DEPTH, CONV_WIDTH, RNN_WIDTH), CONV_WIDTH ** -0.5),
        'conv_b': nrm(ks[9], (DEPTH, RNN_WIDTH), 0.01),
        'w_gate_a': nrm(ks[10], (DEPTH, N_LRU_BLOCKS, LRU_BLOCK, LRU_BLOCK), LRU_BLOCK ** -0.5),
        'b_gate_a': nrm(ks[11], (DEPTH, RNN_WIDTH), 0.01),
        'w_gate_x': nrm(ks[12], (DEPTH, N_LRU_BLOCKS, LRU_BLOCK, LRU_BLOCK), LRU_BLOCK ** -0.5),
        'b_gate_x': nrm(ks[13], (DEPTH, RNN_WIDTH), 0.01),
        'lru_lambda': lru_lambda,
        'g_mlp': gain(ks[14], (DEPTH, D_MODEL)),
        'w_mlp_in': nrm(ks[16], (DEPTH, D_MODEL, D_FF), D_MODEL ** -0.5),
        'w_mlp_out': nrm(ks[17], (DEPTH, D_FF, D_MODEL), D_FF ** -0.5),
        'g_ple': gain(ks[18], (DEPTH, D_MODEL)),
        'w_ple_gate': nrm(ks[19], (DEPTH, D_MODEL, D_MODEL), D_MODEL ** -0.5),
        'w_ple_proj': nrm(ks[20], (DEPTH, PLE_DIM, D_MODEL), PLE_DIM ** -0.5),
        'g_final': gain(ks[21], (D_MODEL,)),
    }

def first_block(x, p, positions, w_in, w_out, g_mix, g_subln, lam_q, lam_k, conv_w, conv_b,
              w_gate_a, b_gate_a, w_gate_x, b_gate_x, lru_lambda, g_mlp, w_mlp_in, w_mlp_out,
              g_ple, w_ple_gate, w_ple_proj, g_final):
    B, S, _ = x.shape
    h = x
    A, R = ATTN_WIDTH, RNN_WIDTH
    for l in range(DEPTH):
        hn = rms_norm(h, g_mix[l])
        proj = hn @ w_in[l]
        q, k, v, xr, gr = jnp.split(proj, [A, 2 * A, 3 * A, 3 * A + R], axis=-1)
        q = partial_rope(q.reshape(B, S, N_DIFF_HEADS, 2, DIFF_HEAD_DIM), positions)
        k = partial_rope(k.reshape(B, S, N_DIFF_HEADS, 2, DIFF_HEAD_DIM), positions)
        v = v.reshape(B, S, N_DIFF_HEADS, V_HEAD_DIM)
        lam_init = 0.8 - 0.6 * math.exp(-0.3 * l)
        dots = jnp.sum(lam_q[l].astype(jnp.float32) * lam_k[l].astype(jnp.float32), axis=-1)
        lam = jnp.exp(dots[0]) - jnp.exp(dots[1]) + lam_init
        o = diff_attention(q, k, v, lam)
        o = (rms_norm(o, g_subln[l]) * (1.0 - lam_init)).reshape(B, S, A)
        xc = causal_depthwise_conv(xr, conv_w[l], conv_b[l])
        y = rg_lru(xc, w_gate_a[l], b_gate_a[l], w_gate_x[l], b_gate_x[l], lru_lambda[l])
        y = y * jax.nn.gelu(gr)
        h = h + jnp.concatenate([o, y], axis=-1) @ w_out[l]
        hm = rms_norm(h, g_mlp[l])
        h = h + jnp.square(jax.nn.relu(hm @ w_mlp_in[l])) @ w_mlp_out[l]
        gate = jax.nn.sigmoid(rms_norm(h, g_ple[l]) @ w_ple_gate[l])
        h = h + gate * (p[l] @ w_ple_proj[l])
    return rms_norm(h, g_final)


CHUNK = 64
POOL_WIDTH = D_MODEL // 2
POOL_WINDOWS = (2, 4, 8, 16)
N_POOL_GROUPS = len(POOL_WINDOWS)
POOL_GROUP = POOL_WIDTH // N_POOL_GROUPS
ATTN_WIDTH_2 = D_MODEL - POOL_WIDTH
HEAD_DIM = 64
N_HEADS = ATTN_WIDTH_2 // HEAD_DIM
ROPE_DIM = HEAD_DIM // 4
IDX_HEADS = 8
IDX_DIM = 64
IDX_ROPE_DIM = IDX_DIM // 4
TOPK_MAX = 256
Q_BLOCK_2 = 64
D_FF_2 = 4 * D_MODEL

SPLITS = (POOL_WIDTH, ATTN_WIDTH_2, ATTN_WIDTH_2, ATTN_WIDTH_2, IDX_HEADS * IDX_DIM, IDX_DIM, IDX_HEADS)
IN_WIDTH_2 = sum(SPLITS)
SPLIT_POINTS = tuple(int(v) for v in np.cumsum(SPLITS)[:-1])


def rms_norm_2(x, g):
    xf = x.astype(jnp.float32)
    y = xf * lax.rsqrt(jnp.mean(xf * xf, axis=-1, keepdims=True) + EPS)
    return (y * g.astype(jnp.float32)).astype(x.dtype)

def rope_partial(x, pos, rot_dim):
    half = rot_dim // 2
    inv = ROPE_THETA ** (-jnp.arange(half, dtype=jnp.float32) / half)
    ang = pos.astype(jnp.float32)[..., None] * inv
    cos = jnp.cos(ang)[:, :, None, :]
    sin = jnp.sin(ang)[:, :, None, :]
    x1 = x[..., :half].astype(jnp.float32)
    x2 = x[..., half:rot_dim].astype(jnp.float32)
    rot = jnp.concatenate([x1 * cos - x2 * sin, x2 * cos + x1 * sin], axis=-1)
    return jnp.concatenate([rot.astype(x.dtype), x[..., rot_dim:]], axis=-1)

def pool_mixer(u, w_pool, pool_scale):
    B, S, _ = u.shape
    ug = u.reshape(B, S, N_POOL_GROUPS, POOL_GROUP)
    cs = jnp.cumsum(ug.astype(jnp.float32), axis=1)
    t = jnp.arange(S)
    outs = []
    for g, w in enumerate(POOL_WINDOWS):
        c = cs[:, :, g]
        lagged = jnp.pad(c, ((0, 0), (w, 0), (0, 0)))[:, :S]
        cnt = jnp.minimum(t + 1, w).astype(jnp.float32)[None, :, None]
        outs.append((c - lagged) / cnt - ug[:, :, g].astype(jnp.float32))
    d = jnp.stack(outs, axis=2).astype(u.dtype)
    y = jnp.einsum('bsgc,gcd->bsgd', d, w_pool)
    return y.reshape(B, S, POOL_WIDTH) * pool_scale

def dsa_attention(q, k, v, iq, ik, iw, topk):
    B, S = q.shape[0], q.shape[1]
    n_blocks = S // Q_BLOCK_2
    key_chunk = jnp.arange(S) // CHUNK
    ik32 = ik.astype(jnp.float32)

    def block(i):
        start = i * Q_BLOCK_2
        qb = lax.dynamic_slice_in_dim(q, start, Q_BLOCK_2, axis=1)
        iqb = lax.dynamic_slice_in_dim(iq, start, Q_BLOCK_2, axis=1).astype(jnp.float32)
        iwb = lax.dynamic_slice_in_dim(iw, start, Q_BLOCK_2, axis=1).astype(jnp.float32)
        q_chunk = (start + jnp.arange(Q_BLOCK_2)) // CHUNK
        allowed = key_chunk[None, :] <= q_chunk[:, None]
        logits = jnp.einsum('bqhd,bsd->bqhs', iqb, ik32) * (IDX_DIM ** -0.5)
        score = jnp.einsum('bqh,bqhs->bqs', iwb, jax.nn.relu(logits))
        score = jnp.where(allowed[None], score, -jnp.inf)
        top_val, top_idx = lax.top_k(score, topk)
        valid = jnp.isfinite(top_val)
        kg = jax.vmap(lambda kk, idx: kk[idx])(k, top_idx)
        vg = jax.vmap(lambda vv, idx: vv[idx])(v, top_idx)
        s = jnp.einsum('bqhd,bqkhd->bqhk', qb.astype(jnp.float32), kg.astype(jnp.float32)) * (HEAD_DIM ** -0.5)
        s = jnp.where(valid[:, :, None, :], s, -jnp.inf)
        p = jax.nn.softmax(s, axis=-1)
        o = jnp.einsum('bqhk,bqkhd->bqhd', p, vg.astype(jnp.float32))
        return o.astype(q.dtype)

    out = lax.map(block, jnp.arange(n_blocks))
    return jnp.transpose(out, (1, 0, 2, 3, 4)).reshape(B, S, N_HEADS * HEAD_DIM)

def second_inputs(seed: int = 0) -> dict:
    key = jax.random.key(seed)
    ks = jax.random.split(key, 12)
    f32 = jnp.float32
    def gain(k):
        return 1.0 + 0.02 * jax.random.normal(k, (DEPTH, D_MODEL), f32)
    x = jax.random.normal(ks[0], (BATCH, SEQ, D_MODEL), f32)
    positions = jnp.broadcast_to(jnp.arange(SEQ, dtype=jnp.int32)[None, :], (BATCH, SEQ)).astype(jnp.int32)
    return {
        "x": x,
        "positions": positions,
        "g_pre_mix": gain(ks[1]),
        "w_in": jax.random.normal(ks[2], (DEPTH, D_MODEL, IN_WIDTH_2), f32) * D_MODEL ** -0.5,
        "w_pool": jax.random.normal(ks[3], (DEPTH, N_POOL_GROUPS, POOL_GROUP, POOL_GROUP), f32) * POOL_GROUP ** -0.5,
        "pool_scale": 1.0 + 0.02 * jax.random.normal(ks[4], (DEPTH, POOL_WIDTH), f32),
        "w_out": jax.random.normal(ks[5], (DEPTH, D_MODEL, D_MODEL), f32) * D_MODEL ** -0.5,
        "g_post_mix": gain(ks[6]),
        "g_pre_ffn": gain(ks[7]),
        "w_ff1": jax.random.normal(ks[8], (DEPTH, D_MODEL, D_FF_2), f32) * D_MODEL ** -0.5,
        "w_ff2": jax.random.normal(ks[9], (DEPTH, D_FF_2, D_MODEL), f32) * D_FF_2 ** -0.5,
        "g_post_ffn": gain(ks[10]),
    }

def second_block(x, positions, g_pre_mix, w_in, w_pool, pool_scale, w_out, g_post_mix,
              g_pre_ffn, w_ff1, w_ff2, g_post_ffn):
    B, S, _ = x.shape
    topk = min(TOPK_MAX, S // 4)
    for l in range(DEPTH):
        h = rms_norm_2(x, g_pre_mix[l])
        proj = h @ w_in[l]
        u_pool, q, k, v, iq, ik, iw = jnp.split(proj, SPLIT_POINTS, axis=-1)
        q = rope_partial(q.reshape(B, S, N_HEADS, HEAD_DIM), positions, ROPE_DIM)
        k = rope_partial(k.reshape(B, S, N_HEADS, HEAD_DIM), positions, ROPE_DIM)
        v = v.reshape(B, S, N_HEADS, HEAD_DIM)
        iq = rope_partial(iq.reshape(B, S, IDX_HEADS, IDX_DIM), positions, IDX_ROPE_DIM)
        ik = rope_partial(ik[:, :, None, :], positions, IDX_ROPE_DIM)[:, :, 0, :]
        iw = iw * (IDX_HEADS ** -0.5)
        a_out = pool_mixer(u_pool, w_pool[l], pool_scale[l])
        b_out = dsa_attention(q, k, v, iq, ik, iw, topk)
        mix = jnp.concatenate([a_out, b_out], axis=-1) @ w_out[l]
        x = x + rms_norm_2(mix, g_post_mix[l])
        h = rms_norm_2(x, g_pre_ffn[l])
        f = jnp.square(jax.nn.relu(h @ w_ff1[l])) @ w_ff2[l]
        x = x + rms_norm_2(f, g_post_ffn[l])
    return x


def setup_inputs(seed=0):
    out = dict(first_inputs(seed))
    for name, value in second_inputs(seed + 1).items():
        if name != "x":
            out[name + "_2"] = value
    return out


def reference(
    x, p, positions, w_in, w_out, g_mix, g_subln, lam_q, lam_k, conv_w, conv_b, w_gate_a,
    b_gate_a, w_gate_x, b_gate_x, lru_lambda, g_mlp, w_mlp_in, w_mlp_out, g_ple, w_ple_gate,
    w_ple_proj, g_final, positions_2, g_pre_mix_2, w_in_2, w_pool_2, pool_scale_2, w_out_2,
    g_post_mix_2, g_pre_ffn_2, w_ff1_2, w_ff2_2, g_post_ffn_2,
):
    x = first_block(
        x, p, positions, w_in, w_out, g_mix, g_subln, lam_q, lam_k, conv_w, conv_b, w_gate_a,
        b_gate_a, w_gate_x, b_gate_x, lru_lambda, g_mlp, w_mlp_in, w_mlp_out, g_ple, w_ple_gate,
        w_ple_proj, g_final,
    )
    return second_block(
        x, positions_2, g_pre_mix_2, w_in_2, w_pool_2, pool_scale_2, w_out_2, g_post_mix_2,
        g_pre_ffn_2, w_ff1_2, w_ff2_2, g_post_ffn_2,
    )


_drawn_inputs = setup_inputs


def setup_inputs(seed=0):
    import zlib

    import numpy as np

    out = dict(_drawn_inputs(seed))
    spreads = {}
    factors = {'lam_q': 2.939,
     'b_gate_a': 47.118,
     'b_gate_x': 24.263,
     'g_ple': 4.136,
     'pool_scale_2': 3.275,
     'g_post_mix_2': 2.8,
     'g_pre_ffn_2': 3.048,
     'g_post_ffn_2': 9.744}
    for name, (base, spread) in spreads.items():
        noise = np.random.default_rng([zlib.crc32(name.encode()), seed]).standard_normal(out[name].shape)
        drawn = base * np.exp(spread * noise) if base else spread * noise
        out[name] = __import__('jax').numpy.asarray(drawn.astype(out[name].dtype))
    for name, factor in factors.items():
        out[name] = (out[name] * factor).astype(out[name].dtype)
    return out
```

```python
import math
from contextlib import ExitStack

import numpy as np

import concourse.bass as bass
from concourse import mybir

F32 = mybir.dt.float32
F32R = mybir.dt.float32r
BF16 = mybir.dt.bfloat16
I32 = mybir.dt.int32
ALU = mybir.AluOpType
ACT = mybir.ActivationFunctionType
AX = mybir.AxisListType

P = 128
D = 1024
S = 512
KT = D // P
QT = S // P
DEPTH = 2
EPS = 1e-6
CW = 256
CHUNK = KT * CW
D_FF = 4 * D
FB = D_FF // D
BC = D // CW
HEADS1 = 4
HEADS2 = 8
DH = 64
TOPK = 128
ROT_HALF = 8
THETA = 500000.0
NEG = -1.0e30
MARK = -3.0e38
WINDOWS = (2, 4, 8, 16)
PAD = 16
CONV = 4

A_XR, A_GR, A_Q, A_K, A_V = 0, 2, 4, 6, 8
A_OUT = 10
A_PROJ = A_OUT + BC
A_MLP = A_PROJ + 1
A_GATE = A_MLP + 2 * BC * FB
A_CHUNKS = A_GATE + BC
B_IQ, B_IKW, B_U, B_Q, B_K, B_V = 0, 2, 3, 5, 7, 9
B_OUT = 11
B_FF = B_OUT + BC
B_CHUNKS = B_FF + 2 * BC * FB

AP_GMIX, AP_GMLP, AP_GPLE, AP_GSUB = 0, 8, 16, 24
AP_CONVW, AP_CONVB, AP_BA, AP_BX, AP_LRU = 25, 41, 45, 49, 53
AP_LAMQ, AP_LAMK, AP_INIT, AP_REST = 57, 185, 313, 314
AP_N = 315
BP_GPRE, BP_GPOST, BP_FPRE, BP_FPOST, BP_SCALE, BP_WPOOL = 0, 8, 16, 24, 32, 36
BP_N = BP_WPOOL + 4 * P
C_ID, C_ONES, C_TRI, C_CHUNK, C_FREQ, C_SIGN, C_CNT, C_GFIN, C_HPI, C_MHALF = 0, 128, 256, 384, 512, 513, 514, 578, 586, 587
C_N = C_MHALF + QT

TWO_PI = (1608.0 / 2**8, 254.0 / 2**17, -172.0 / 2**26)
TWO_PI += (2 * math.pi - sum(TWO_PI),)
ROUND = 1.5 * 2.0**23
PI_BELOW = 3.1415925


class Steps:

    def __init__(self, engine, semaphore):
        self.engine, self.semaphore, self.count = engine, semaphore, 0

    def mark(self, instruction):
        instruction.then_inc(self.semaphore, 1)
        self.count += 1

    def settle(self):
        self.engine.wait_ge(self.semaphore, self.count)


class Memory:
    pass


def build(nc, weights_a, weights_b, params_a, params_b, gates, embed, constants, positions, xt, out):
    with ExitStack() as ctx:
        def sb(name, shape, dtype=F32):
            return ctx.enter_context(nc.sbuf_tensor(name, shape, dtype))

        mem = Memory()
        mem.x = sb("x", [P, KT, S])
        mem.gh = sb("gh", [P, KT, S], F32R)
        mem.gl = sb("gl", [P, KT, S], F32R)
        mem.hh = sb("hh", [P, KT, S], F32R)
        mem.hl = sb("hl", [P, KT, S], F32R)
        mem.wr = sb("wr", [P, 2, CHUNK])
        mem.wh = sb("wh", [P, 2, CHUNK], F32R)
        mem.wl = sb("wl", [P, 2, CHUNK], F32R)
        mem.cst = sb("cst", [P, C_N])
        mem.par = sb("par", [P, max(AP_N, BP_N)])
        mem.rb = sb("rb", [P, S])
        mem.sq = sb("sq", [P, 2, S])
        mem.tmp = sb("tmp", [P, 4, S])
        mem.small = sb("small", [P, 256])
        mem.idb = sb("idb", [P, P], BF16)
        at = nc.sbuf_base
        mem.arena = sb("arena", [P, ARENA])
        mem.praw = nc.alloc_sbuf_tensor_at("praw", [P, 2, S], F32, offset=at + 4 * A1_XC)
        mem.ph = nc.alloc_sbuf_tensor_at("ph", [P, 2, S], F32R, offset=at + 4 * (A1_XC + 2 * S))
        mem.pl = nc.alloc_sbuf_tensor_at("pl", [P, 2, S], F32R, offset=at + 4 * (A1_XC + 4 * S))
        mem.ps = ctx.enter_context(nc.psum_tensor("ps", [P, 8, S], F32))

        prologue(nc, mem, constants, xt)
        with nc.Fori(0, DEPTH) as layer:
            first_stack_layer(nc, mem, layer, weights_a, params_a, gates, embed, positions[0:P, :])
        final_norm(nc, mem)
        with nc.Fori(0, DEPTH) as layer:
            second_stack_layer(nc, mem, layer, weights_b, params_b, positions[P:2 * P, :])
        epilogue(nc, mem, out)


def semaphores(nc, ctx, names):
    made = {name: ctx.enter_context(nc.semaphore(name)) for name in names.split()}
    numbers = [s.num for s in made.values()]
    assert numbers == list(range(numbers[0], numbers[-1] + 1))
    return made, range(numbers[0], numbers[-1] + 1)


def clear(nc, used):
    nc.gpsimd.sem_clear(used)
    nc.all_engine_barrier()


A1_QK, A1_XR, A1_CR, A1_XC = 0, 4096, 4096 + 2064, 4096 + 2064 + 1024
A1_R, A1_I, A1_GR = A1_XC + 2048, A1_XC + 4096, A1_XC + 6144
A1_GW = A1_QK + 6 * S
ARENA = 15392


def prologue(nc, mem, constants, xt):
    with ExitStack() as ctx:
        sem, used = semaphores(nc, ctx, "loaded cast")
        with nc.Block() as block:
            @block.sync
            def _(sp):
                sp.dma_start(mem.cst[:, :], constants).then_inc(sem["loaded"], 16)
                sp.dma_start(mem.x[:, :, :], xt.rearrange("(k p) s -> p k s", p=P)).then_inc(sem["loaded"], 16)
                sp.wait_ge(sem["loaded"], 32)

            @block.vector
            def _(dve):
                dve.wait_ge(sem["loaded"], 32)
                dve.tensor_copy(mem.idb[:, :], mem.cst[:, C_ID:C_ID + P]).then_inc(sem["cast"], 1)
        clear(nc, used)


def epilogue(nc, mem, out):
    with ExitStack() as ctx:
        sem, used = semaphores(nc, ctx, "stored")
        with nc.Block() as block:
            @block.sync
            def _(sp):
                sp.dma_start(out.rearrange("(k p) s -> p k s", p=P), mem.x[:, :, :]).then_inc(sem["stored"], 16)
                sp.wait_ge(sem["stored"], 16)


def final_norm(nc, mem):
    x, sq, ps, cst, small, tmp = mem.x, mem.sq, mem.ps, mem.cst, mem.small, mem.tmp
    stat, ms, rs = ps[:, 4, 0:QT], small[:, 0:QT], small[:, QT:2 * QT]
    with ExitStack() as ctx:
        sem, used = semaphores(nc, ctx, "squared summed mean root diag spread scaled")
        with nc.Block() as block:
            @block.scalar
            def _(act):
                for k in range(KT):
                    if k >= 2:
                        act.wait_ge(sem["summed"], k - 1)
                    act.activation(sq[:, k % 2, :], x[:, k, :], ACT.Square).then_inc(sem["squared"], 1)

            @block.tensor
            def _(pe):
                for k in range(KT):
                    pe.wait_ge(sem["squared"], k + 1)
                    for i in range(QT):
                        last = pe.matmul(stat[:, i:i + 1], sq[:, k % 2, i * P:(i + 1) * P], cst[:, C_ONES:C_ONES + 1],
                                         start=(k == 0 and i == 0), stop=(k == KT - 1), skip_group_check=True)
                    last.then_inc(sem["summed"], 1)
                pe.wait_ge(sem["diag"], 1)
                pe.matmul(ps[:, 5, :], cst[:, C_ONES:C_ONES + P], tmp[:, 3, :], start=True, stop=True).then_inc(sem["spread"], 1)

            @block.gpsimd
            def _(pool):
                pool.wait_ge(sem["mean"], 1)
                pool.tensor_tensor(rs, ms, cst[:, C_MHALF:C_MHALF + QT], ALU.pow).then_inc(sem["root"], 1)

            @block.vector
            def _(dve):
                dve.wait_ge(sem["summed"], KT)
                dve.tensor_scalar(ms, stat, 1.0 / D, EPS, ALU.mult, ALU.add).then_inc(sem["mean"], 1)
                dve.wait_ge(sem["root"], 1)
                diagonals(dve, mem, rs).then_inc(sem["diag"], 1)
                dve.wait_ge(sem["spread"], 1)
                for k in range(KT):
                    dve.scalar_tensor_tensor(out=x[:, k, :], in0=x[:, k, :], scalar=cst[:, C_GFIN + k:C_GFIN + k + 1],
                                             in1=ps[:, 5, :], op0=ALU.mult, op1=ALU.mult).then_inc(sem["scaled"], 1)
        clear(nc, used)


def diagonals(dve, mem, rs):
    return dve.tensor_tensor(mem.tmp[:, 3, :].rearrange("p (i c) -> p i c", i=QT),
                             mem.cst[:, C_ID:C_ID + P].unsqueeze(1).broadcast_to([P, QT, P]),
                             rs.unsqueeze(2).broadcast_to([P, QT, P]), ALU.mult)



def once(_):
    return 0


def load_chunk(sp, mem, sem, weights, row, c, per=once):
    row = sp.snap(row)
    if c >= 2:
        sp.wait_ge(sem["low"], c - 1 + per(2 * BC))
    loaded = (sem["loaded0"], sem["loaded1"])[c % 2]
    sp.dma_start(mem.wr[:, c % 2, :], weights[bass.ds(row, P), :]).then_inc(loaded, 16)


def split_high(act, mem, sem, c, used, per=once):
    act.wait_ge((sem["loaded0"], sem["loaded1"])[c % 2], 16 * (c // 2 + 1) + per(16 * BC))
    if c >= 2:
        act.wait_ge(sem["product"], used + per(4 * BC))
    act.activation(mem.wh[:, c % 2, :], mem.wr[:, c % 2, :], ACT.Copy).then_inc(sem["high"], 1)


def split_low(dve, mem, sem, c, per=once):
    dve.wait_ge(sem["high"], c + 1 + per(2 * BC))
    dve.tensor_tensor(mem.wl[:, c % 2, :], mem.wr[:, c % 2, :], mem.wh[:, c % 2, :].bitcast(F32),
                      ALU.subtract).then_inc(sem["low"], 1)


def three_passes(pe, out, w_high, w_low, high, low, first, last, swap=False):
    pairs = ((w_high, high), (w_high, low), (w_low, high))
    if swap:
        pairs = ((high, w_high), (low, w_high), (high, w_low))
    for n, (stationary, moving) in enumerate(pairs):
        done = pe.matmul(out, stationary, moving, start=(first and n == 0), stop=(last and n == 2),
                         skip_group_check=True)
    return done


def product_tile(pe, mem, sem, c, column, tile, high, low, order=range(KT), before=None, width=P, per=once):
    if column == 0:
        pe.wait_ge(sem["low"], c + 1 + per(2 * BC))
    if tile >= 4:
        pe.wait_ge(sem["drained"], tile - 3 + per(4 * BC))
    wh = mem.wh[:, c % 2, :].rearrange("p (k n) -> p k n", k=KT)
    wl = mem.wl[:, c % 2, :].rearrange("p (k n) -> p k n", k=KT)
    order = list(order)
    for k in order:
        if before:
            before(k)
        last = three_passes(pe, mem.ps[0:width, tile % 4, :], wh[:, k, column:column + width], wl[:, k, column:column + width],
                            high[:, k, :], low[:, k, :], k == order[0], k == order[-1])
    last.then_inc(sem["product"], 1)


def token_tile(pe, mem, sem, c, i, tile):
    if i == 0:
        pe.wait_ge(sem["low"], c + 1)
    pe.wait_ge(sem["drained"], tile - 3)
    wh = mem.wh[:, c % 2, :].rearrange("p (k n) -> p k n", k=KT)
    wl = mem.wl[:, c % 2, :].rearrange("p (k n) -> p k n", k=KT)
    for k in range(KT):
        last = three_passes(pe, mem.ps[:, tile % 4, 0:CW], wh[:, k, :], wl[:, k, :],
                            mem.gh[:, k, i * P:(i + 1) * P], mem.gl[:, k, i * P:(i + 1) * P], k == 0, k == KT - 1, swap=True)
    last.then_inc(sem["product"], 1)



def square_slice(act, mem, sem, n, k, source):
    if KT * n + k >= 2:
        act.wait_ge(sem["summed"], KT * n + k - 1)
    act.activation(mem.sq[:, k % 2, :], source[:, k, :], ACT.Square).then_inc(sem["squared"], 1)


def sum_slice(pe, mem, sem, n, k):
    pe.wait_ge(sem["squared"], KT * n + k + 1)
    if n and k == 0:
        pe.wait_ge(sem["mean"], n)
    for i in range(QT):
        last = pe.matmul(mem.ps[:, 4, i:i + 1], mem.sq[:, k % 2, i * P:(i + 1) * P], mem.cst[:, C_ONES:C_ONES + 1],
                         start=(k == 0 and i == 0), stop=(k == KT - 1), skip_group_check=True)
    last.then_inc(sem["summed"], 1)


def mean_square(dve, mem, sem, n):
    dve.wait_ge(sem["summed"], KT * (n + 1))
    dve.tensor_scalar(mem.small[:, 0:QT], mem.ps[:, 4, 0:QT], 1.0 / D, EPS, ALU.mult, ALU.add).then_inc(sem["mean"], 1)


def one_over_root(pool, mem, sem, n):
    pool.wait_ge(sem["mean"], n + 1)
    pool.tensor_tensor(mem.small[:, QT:2 * QT], mem.small[:, 0:QT], mem.cst[:, C_MHALF:C_MHALF + QT],
                       ALU.pow).then_inc(sem["root"], 1)


def root_diagonals(dve, mem, sem, n):
    dve.wait_ge(sem["root"], n + 1)
    diagonals(dve, mem, mem.small[:, QT:2 * QT]).then_inc(sem["diag"], 1)


def spread_root(pe, mem, sem, n):
    pe.wait_ge(sem["diag"], n + 1)
    pe.matmul(mem.ps[:, 5, :], mem.cst[:, C_ONES:C_ONES + P], mem.tmp[:, 3, :], start=True, stop=True).then_inc(sem["spread"], 1)


def keep_root(act, mem, sem, n):
    act.wait_ge(sem["spread"], n + 1)
    act.activation(mem.rb[:, :], mem.ps[:, 5, :], ACT.Copy).then_inc(sem["kept"], 1)


def gain_high(act, mem, sem, k, gains):
    act.activation(mem.gh[:, k, :], mem.x[:, k, :], ACT.Copy, scale=mem.par[:, gains + k:gains + k + 1]).then_inc(sem["gain_high"], 1)


def gain_low(dve, mem, sem, n, k, gains):
    dve.wait_ge(sem["gain_high"], KT * n + k + 1)
    dve.scalar_tensor_tensor(out=mem.gl[:, k, :], in0=mem.x[:, k, :], scalar=mem.par[:, gains + k:gains + k + 1],
                             in1=mem.gh[:, k, :].bitcast(F32), op0=ALU.mult, op1=ALU.subtract).then_inc(sem["gain_low"], 1)



def rotary_angles(dve, steps, mem, whole, left):
    freq = mem.cst[:, C_FREQ:C_FREQ + 1]
    steps.mark(dve.tensor_copy(left, whole.bitcast(I32)))
    steps.settle()
    steps.mark(dve.tensor_scalar(left, left, freq, None, ALU.mult))
    steps.settle()
    steps.mark(dve.tensor_scalar(whole, left, 1.0 / (2 * math.pi), ROUND, ALU.mult, ALU.add))
    steps.settle()
    steps.mark(dve.tensor_scalar(whole, whole, ROUND, None, ALU.subtract))
    for part in TWO_PI:
        steps.settle()
        steps.mark(dve.scalar_tensor_tensor(out=left, in0=whole, scalar=-part, in1=left, op0=ALU.mult, op1=ALU.add))
    steps.settle()
    steps.mark(dve.tensor_scalar(left, left, PI_BELOW, -PI_BELOW, ALU.min, ALU.max))
    steps.settle()
    return dve.scalar_tensor_tensor(out=whole, in0=left, scalar=-1.0, in1=left, op0=ALU.mult, op1=ALU.max)


SWAP = [(i + ROT_HALF) % (2 * ROT_HALF) if i < 2 * ROT_HALF else i for i in range(32)]


def rotate(dve, steps, mem, sem, tile, out, cos, sin, width=P):
    dve.wait_ge(sem["product"], tile + 1)
    acc = mem.ps[0:width, tile % 4, :]
    steps.settle()
    steps.mark(dve.stream_shuffle(mem.tmp[0:width, 2, :], acc, SWAP))
    dve.tensor_tensor(out, acc, cos[0:width], ALU.mult).then_inc(sem["drained"], 1)
    steps.settle()
    steps.mark(dve.tensor_tensor(mem.tmp[0:width, 2, :], mem.tmp[0:width, 2, :], sin[0:width], ALU.mult))
    steps.settle()
    dve.wait_ge(sem["drained"], tile + 1)
    steps.mark(dve.tensor_tensor(out, out, mem.tmp[0:width, 2, :], ALU.add))



A_TILE = {c: 2 * c for c in range(A_V)}
A_TILE.update({A_V: 16, A_V + 1: 20, A_V + 2: 24})
A_TILE.update({c: 24 + 2 * (c - A_OUT) for c in range(A_OUT, A_PROJ + 1)})
A_TILE.update({c: 40 + 2 * (c - A_MLP) for c in range(A_MLP, A_CHUNKS + 1)})

SM_OMS, SM_ORS, SM_C8, SM_NC8, SM_X, SM_E, SM_S, SM_S2, SM_PL, SM_LAM, SM_GS = 8, 12, 16, 20, 24, 28, 32, 36, 40, 44, 50
SM_MAX, SM_NEG, SM_SUM, SM_INV = 56, 60, 64, 68
LOG1P = (1 / 17, 1 / 15, 1 / 13, 1 / 11, 1 / 9, 1 / 7, 1 / 5, 1 / 3, 1.0)


def a_used(c):
    return A_TILE[c - 1]


def first_stack_layer(nc, mem, layer, weights, params, gates, embed, positions):
    ar, ps, cst, par, small, tmp, x = mem.arena, mem.ps, mem.cst, mem.par, mem.small, mem.tmp, mem.x
    qk = ar[:, A1_QK:A1_QK + 4096].rearrange("p (t s) -> p t s", s=S)
    xr = ar[:, A1_XR:A1_XR + 4 * (S + 4)].rearrange("p (t s) -> p t s", s=S + 4)
    v = ar[:, A1_XR:A1_XR + 4 * S].rearrange("p (t s) -> p t s", s=S)
    cos, sin = ar[:, A1_CR:A1_CR + S], ar[:, A1_CR + S:A1_CR + 2 * S]
    xc, rr, ii, gr = (ar[:, a:a + 2048].rearrange("p (t s) -> p t s", s=S) for a in (A1_XC, A1_R, A1_I, A1_GR))
    gw = ar[:, A1_GW:A1_GW + 2 * S].rearrange("p (g t n) -> p g t n", g=2, t=4)
    prob = ar[:, A1_XC:A1_XC + 2048].rearrange("p (b c s) -> p b c s", b=2, c=2)
    mixed = ar[:, A1_R:A1_R + 1024].rearrange("p (b s) -> p b s", b=2)
    head_out = ar[:, A1_R + 1024:A1_R + 2048].rearrange("p (b s) -> p b s", b=2)
    pt = ar[:, A1_I:A1_I + 4096].rearrange("p (b k s) -> p b k s", b=2, k=QT)
    proj = qk
    ident, ones = cst[:, C_ID:C_ID + P], cst[:, C_ONES:C_ONES + P]
    STEPS = 4 * HEADS1

    with ExitStack() as ctx:
        sem, used = semaphores(nc, ctx, (
            "loaded0 loaded1 vectors positioned embedded high low product drained squared summed mean root diag spread kept "
            "gain_high gain_low own act_own tables softexp lamexp conv gate_product gated gelued gated_input decayed gain_ready "
            "rooted y_ready y_high y_low scored maxed exped mixed_done turned untangled weighted copied o_squared o_summed o_mean o_root "
            "o_diag o_spread o_ready o_high o_low embed_high embed_low hidden hidden_high hidden_low gate_in gate_out padded"))
        with nc.Block() as block:

            @block.sync
            def _(sp):
                def chunk(c, per=once, j=None):
                    row = (layer * A_CHUNKS + c) * P if j is None else (layer * A_CHUNKS + c + j * (2 * BC)) * P
                    load_chunk(sp, mem, sem, weights, row, c, per)

                rows = sp.snap(layer * P)
                sp.dma_start(par[:, 0:AP_N], params[bass.ds(rows, P), :]).then_inc(sem["vectors"], 16)
                chunk(0)
                chunk(1)
                sp.dma_start(tmp[:, 0, :].bitcast(I32), positions).then_inc(sem["positioned"], 16)
                sp.dma_start(ar[:, A1_GW:A1_GW + 2 * S], gates[bass.ds(rows, P), :]).then_inc(sem["positioned"], 16)
                for c in range(2, A_OUT + 2):
                    chunk(c)
                sp.wait_ge(sem["copied"], HEADS1)
                sp.dma_start(mem.praw[:, :, :].rearrange("p k s -> p (k s)"), embed[bass.ds(rows, P), :]).then_inc(sem["embedded"], 16)
                for c in range(A_OUT + 2, A_MLP):
                    chunk(c)
                with sp.Fori(0, FB) as j:
                    for i in range(2 * BC):
                        chunk(A_MLP + i, lambda n: j * n, j)
                for c in range(A_GATE, A_CHUNKS):
                    chunk(c)

            @block.gpsimd
            def _(pool):
                pool.memset(xr[:, :, 0:4], 0.0).then_inc(sem["padded"], 1)
                one_over_root(pool, mem, sem, 0)
                for t in range(4):
                    pool.wait_ge(sem["gated"], 2 * (t + 1))
                    pool.tensor_tensor(xc[:, t, :], xc[:, t, :], ii[:, t, :], ALU.mult).then_inc(sem["gated_input"], 1)
                for h in range(HEADS1):
                    pool.wait_ge(sem["o_mean"], h + 1)
                    pool.tensor_tensor(small[:, SM_ORS:SM_ORS + QT], small[:, SM_OMS:SM_OMS + QT],
                                       cst[:, C_MHALF:C_MHALF + QT], ALU.pow).then_inc(sem["o_root"], 1)
                for n in (1, 2):
                    one_over_root(pool, mem, sem, n)

            @block.scalar
            def _(act):
                act.wait_ge(sem["vectors"], 16)
                for k in range(KT):
                    square_slice(act, mem, sem, 0, k, x)
                    gain_high(act, mem, sem, k, AP_GMIX)
                split_high(act, mem, sem, 0, 0)
                split_high(act, mem, sem, 1, 0)
                keep_root(act, mem, sem, 0)
                act.wait_ge(sem["softexp"], 1)
                act.activation(small[:, SM_E:SM_E + 4], small[:, SM_X:SM_X + 4], ACT.Exp, scale=-1.0).then_inc(sem["act_own"], 1)
                act.activation(small[:, SM_LAM + 2:SM_LAM + 4], small[:, SM_LAM:SM_LAM + 2], ACT.Exp).then_inc(sem["lamexp"], 1)
                split_high(act, mem, sem, 2, a_used(2))
                split_high(act, mem, sem, 3, a_used(3))
                act.wait_ge(sem["tables"], 1)
                act.activation(sin, tmp[:, 1, :], ACT.Sin, scale=cst[:, C_SIGN:C_SIGN + 1]).then_inc(sem["tables"], 1)
                act.activation(cos, tmp[:, 0, :], ACT.Sin, scale=-1.0, bias=cst[:, C_HPI:C_HPI + 1]).then_inc(sem["tables"], 1)
                for t in range(4):
                    for g, (gate, bias) in enumerate(((rr, AP_BA), (ii, AP_BX))):
                        act.wait_ge(sem["gate_product"], 2 * t + g + 1)
                        act.activation(gate[:, t, :], ps[:, 6 + g, :], ACT.Sigmoid,
                                       bias=par[:, bias + t:bias + t + 1]).then_inc(sem["gated"], 1)
                split_high(act, mem, sem, 4, a_used(4))
                for t in range(4):
                    act.wait_ge(sem["drained"], A_TILE[A_GR] + t + 1)
                    act.activation(gr[:, t, :], gr[:, t, :], ACT.Gelu_apprx_tanh).then_inc(sem["gelued"], 1)
                split_high(act, mem, sem, 5, a_used(5))
                for t in range(4):
                    act.wait_ge(sem["gated_input"], t + 1)
                    act.wait_ge(sem["gated"], 8)
                    act.activation(ii[:, t, :], rr[:, t, :], ACT.Tanh, scale=small[:, SM_C8 + t:SM_C8 + t + 1]).then_inc(sem["decayed"], 1)
                    act.activation(rr[:, t, :], rr[:, t, :], ACT.Exp, scale=small[:, SM_NC8 + t:SM_NC8 + t + 1]).then_inc(sem["decayed"], 1)
                split_high(act, mem, sem, 6, a_used(6))
                for t in range(4):
                    if t >= 2:
                        act.wait_ge(sem["gain_ready"], t - 1)
                    act.wait_ge(sem["decayed"], 2 * t + 2)
                    act.wait_ge(sem["summed"], KT)
                    act.activation(mem.sq[:, t % 2, :], rr[:, t, :], ACT.Square).then_inc(sem["decayed"], 1)
                split_high(act, mem, sem, 7, a_used(7))
                for t in range(4):
                    act.wait_ge(sem["gain_ready"], t + 1)
                    act.activation(ii[:, t, :], ii[:, t, :], ACT.Sqrt).then_inc(sem["rooted"], 1)
                split_high(act, mem, sem, 8, a_used(8))
                split_high(act, mem, sem, 9, a_used(9))
                for t in range(4):
                    act.wait_ge(sem["y_ready"], t + 1)
                    act.activation(mem.hh[:, 4 + t, :], tmp[:, 1, :], ACT.Copy).then_inc(sem["y_high"], 1)

                def exponents(s):
                    h, i = divmod(s, QT)
                    n = P * (i + 1)
                    act.wait_ge(sem["maxed"], s + 1)
                    if s == 0:
                        act.wait_ge(sem["y_low"], 4)
                    if s >= 2:
                        act.wait_ge(sem["mixed_done"], s - 1)
                    for c in range(2):
                        act.activation(prob[:, s % 2, c, 0:n], ps[:, 2 * (s % 2) + c, 0:n], ACT.Exp, scale=DH ** -0.5,
                                       bias=small[:, SM_NEG + 2 * (s % 2) + c:SM_NEG + 2 * (s % 2) + c + 1],
                                       accum_out=small[:, SM_SUM + 2 * (s % 2) + c:SM_SUM + 2 * (s % 2) + c + 1]).then_inc(sem["exped"], 1)

                def untangle(s):
                    h, i = divmod(s, QT)
                    act.wait_ge(sem["turned"], s + 1)
                    if h >= 2:
                        act.wait_ge(sem["weighted"], h - 1)
                    act.activation(pt[:, h % 2, 0:i + 1, P * i:P * (i + 1)],
                                   ps[:, 5, 0:P * (i + 1)].rearrange("p (k q) -> p k q", q=P), ACT.Copy).then_inc(sem["untangled"], 1)

                def head_squares(h):
                    act.wait_ge(sem["weighted"], h + 1)
                    if h >= 2:
                        act.wait_ge(sem["o_ready"], h - 1)
                        act.wait_ge(sem["o_summed"], h - 1)
                    act.activation(head_out[:, h % 2, :], ps[:, 6, :], ACT.Copy).then_inc(sem["copied"], 1)
                    act.activation(mem.sq[:, h % 2, :], ps[:, 6, :], ACT.Square).then_inc(sem["o_squared"], 1)

                def head_high(h):
                    act.wait_ge(sem["o_ready"], h + 1)
                    act.activation(mem.hh[:, h, :], tmp[:, 1, :], ACT.Copy).then_inc(sem["o_high"], 1)

                exponents(0)
                for s in range(STEPS):
                    if s + 1 < STEPS:
                        exponents(s + 1)
                    h, i = divmod(s, QT)
                    if h and i == 0:
                        head_squares(h - 1)
                    untangle(s)
                    if h and i == 2:
                        head_high(h - 1)
                    if s == 8:
                        split_high(act, mem, sem, A_OUT, a_used(A_OUT))
                        split_high(act, mem, sem, A_OUT + 1, a_used(A_OUT + 1))
                head_squares(HEADS1 - 1)
                head_high(HEADS1 - 1)

                def own_slice(n, k, tile, gains):
                    act.wait_ge(sem["drained"], tile + 1)
                    square_slice(act, mem, sem, n, k, x)
                    gain_high(act, mem, sem, k, gains)

                for c in range(A_OUT, A_PROJ):
                    if c + 1 >= A_OUT + 2:
                        split_high(act, mem, sem, c + 1, a_used(c + 1))
                    for t in range(2):
                        k = 2 * (c - A_OUT) + t
                        own_slice(1, k, A_TILE[c] + t, AP_GMLP)
                    if c == A_OUT:
                        act.wait_ge(sem["embedded"], 16)
                        act.wait_ge(sem["o_low"], HEADS1)
                        act.activation(mem.ph[:, :, :], mem.praw[:, :, :], ACT.Copy).then_inc(sem["embed_high"], 1)
                split_high(act, mem, sem, A_MLP, a_used(A_MLP))
                keep_root(act, mem, sem, 1)

                def mlp_first(c0, per, j):
                    for i in range(BC):
                        split_high(act, mem, sem, c0 + i + 1, a_used(c0 + i + 1), per)
                        for t in range(2):
                            act.wait_ge(sem["hidden"], 2 * i + t + 1 + j * KT)
                            act.activation(mem.hh[:, 2 * i + t, :], tmp[:, 1, :], ACT.Copy).then_inc(sem["hidden_high"], 1)

                with act.Fori(0, FB - 1) as j:
                    def per(n):
                        return j * n

                    mlp_first(A_MLP, per, j)
                    for i in range(BC, 2 * BC):
                        split_high(act, mem, sem, A_MLP + i + 1, a_used(A_MLP + i + 1), per)
                c0 = A_GATE - 2 * BC
                mlp_first(c0, once, FB - 1)
                for c in range(c0 + BC, A_GATE):
                    split_high(act, mem, sem, c + 1, a_used(c + 1))
                    for t in range(2):
                        own_slice(2, 2 * (c - c0 - BC) + t, A_TILE[c] + t, AP_GPLE)
                keep_root(act, mem, sem, 2)
                for c in range(A_GATE, A_CHUNKS):
                    if c + 1 < A_CHUNKS:
                        split_high(act, mem, sem, c + 1, a_used(c + 1))
                    for t in range(2):
                        act.wait_ge(sem["drained"], A_TILE[c] + t + 1)
                        act.activation(tmp[:, 1, :], tmp[:, 0, :], ACT.Sigmoid).then_inc(sem["gate_out"], 1)

            @block.vector
            def _(dve):
                own = Steps(dve, sem['own'])
                dve.wait_ge(sem["vectors"], 16)
                for k in range(KT):
                    gain_low(dve, mem, sem, 0, k, AP_GMIX)
                split_low(dve, mem, sem, 0)
                mean_square(dve, mem, sem, 0)
                root_diagonals(dve, mem, sem, 0)
                split_low(dve, mem, sem, 1)

                sx, se, ss, s2, spl = (small[:, a:a + 4] for a in (SM_X, SM_E, SM_S, SM_S2, SM_PL))
                lru = par[:, AP_LRU:AP_LRU + 4]
                own.mark(dve.scalar_tensor_tensor(out=sx, in0=lru, scalar=-1.0, in1=lru, op0=ALU.mult, op1=ALU.max))
                dots = tmp[:, 3, 0:2 * DH]
                dve.wait_ge(sem["spread"], 1)
                own.mark(dve.tensor_tensor(dots, par[:, AP_LAMQ:AP_LAMQ + 2 * DH], par[:, AP_LAMK:AP_LAMK + 2 * DH], ALU.mult))
                own.settle()
                dve.tensor_reduce(small[:, SM_LAM:SM_LAM + 2], dots.rearrange("p (a d) -> p a d", a=2), AX.X, ALU.add)\
                    .then_inc(sem["softexp"], 1)
                dve.wait_ge(sem["act_own"], 1)
                dve.wait_ge(sem["lamexp"], 1)
                own.mark(dve.tensor_scalar(ss, se, 2.0, None, ALU.add))
                own.settle()
                own.mark(dve.reciprocal(ss, ss))
                own.settle()
                own.mark(dve.tensor_tensor(ss, ss, se, ALU.mult))
                own.settle()
                own.mark(dve.tensor_tensor(s2, ss, ss, ALU.mult))
                own.settle()
                own.mark(dve.tensor_scalar(spl, s2, LOG1P[0], None, ALU.mult))
                for term in LOG1P[1:-1]:
                    own.settle()
                    own.mark(dve.scalar_tensor_tensor(out=spl, in0=spl, scalar=term, in1=s2, op0=ALU.add, op1=ALU.mult))
                own.settle()
                own.mark(dve.scalar_tensor_tensor(out=spl, in0=spl, scalar=1.0, in1=ss, op0=ALU.add, op1=ALU.mult))
                own.mark(dve.tensor_scalar(sx, lru, -1.0, 0.0, ALU.mult, ALU.max))
                own.settle()
                own.mark(dve.scalar_tensor_tensor(out=spl, in0=spl, scalar=2.0, in1=sx, op0=ALU.mult, op1=ALU.add))
                own.settle()
                own.mark(dve.tensor_scalar(small[:, SM_C8:SM_C8 + 4], spl, 8.0, None, ALU.mult))
                own.mark(dve.tensor_scalar(small[:, SM_NC8:SM_NC8 + 4], spl, -8.0, None, ALU.mult))
                nlam = small[:, SM_LAM + 4:SM_LAM + 5]
                own.mark(dve.tensor_tensor(nlam, small[:, SM_LAM + 3:SM_LAM + 4], small[:, SM_LAM + 2:SM_LAM + 3], ALU.subtract))
                own.settle()
                own.mark(dve.tensor_scalar(nlam, nlam, par[:, AP_INIT:AP_INIT + 1], None, ALU.subtract))
                gsub = small[:, SM_GS:SM_GS + 1]
                own.mark(dve.tensor_scalar(gsub, par[:, AP_GSUB:AP_GSUB + 1], par[:, AP_REST:AP_REST + 1], None, ALU.mult))

                def drain(out, tile):
                    dve.wait_ge(sem["product"], tile + 1)
                    dve.tensor_tensor(out, ps[:, tile % 4, :], mem.rb[:, :], ALU.mult).then_inc(sem["drained"], 1)

                def convolve(t):
                    for tap in range(CONV - 1, -1, -1):
                        taps = par[:, AP_CONVW + 4 * tap + t:AP_CONVW + 4 * tap + t + 1]
                        window = xr[:, t, 1 + tap:1 + tap + S]
                        if tap == CONV - 1:
                            own.mark(dve.tensor_scalar(xc[:, t, :], window, taps, par[:, AP_CONVB + t:AP_CONVB + t + 1], ALU.mult, ALU.add))
                            own.settle()
                            continue
                        last = dve.scalar_tensor_tensor(out=xc[:, t, :], in0=window, scalar=taps, in1=xc[:, t, :],
                                                        op0=ALU.mult, op1=ALU.add)
                        if tap:
                            own.mark(last)
                            own.settle()
                    last.then_inc(sem["conv"], 1)

                dve.wait_ge(sem["kept"], 1)
                dve.wait_ge(sem["padded"], 1)
                for c in (A_XR, A_XR + 1):
                    for t in range(2):
                        drain(xr[:, 2 * c + t, 4:4 + S], A_TILE[c] + t)
                    if c == 0:
                        split_low(dve, mem, sem, 2)
                        dve.wait_ge(sem["positioned"], 32)
                        rotary_angles(dve, own, mem, tmp[:, 0, :], tmp[:, 1, :]).then_inc(sem["tables"], 1)
                    for t in range(2):
                        dve.wait_ge(sem["drained"], A_TILE[c] + t + 1)
                        convolve(2 * c + t)
                for c in (A_GR, A_GR + 1):
                    split_low(dve, mem, sem, c + 1)
                    for t in range(2):
                        drain(gr[:, 2 * (c - A_GR) + t, :], A_TILE[c] + t)
                dve.wait_ge(sem["tables"], 3)
                own.mark(dve.tensor_tensor(sin, sin, mem.rb[:, :], ALU.mult))
                own.mark(dve.tensor_tensor(cos, cos, mem.rb[:, :], ALU.mult))
                own.settle()

                def gain(t):
                    dve.wait_ge(sem["decayed"], 8 + t + 1)
                    dve.scalar_tensor_tensor(out=ii[:, t, :], in0=mem.sq[:, t % 2, :], scalar=1.0, in1=ii[:, t, :],
                                             op0=ALU.add, op1=ALU.mult).then_inc(sem["gain_ready"], 1)

                def recur(t):
                    dve.wait_ge(sem["rooted"], t + 1)
                    dve.wait_ge(sem["gated_input"], t + 1)
                    own.mark(dve.tensor_tensor(xc[:, t, :], xc[:, t, :], ii[:, t, :], ALU.mult))
                    own.settle()
                    own.mark(dve.tensor_tensor_scan(ii[:, t, :], rr[:, t, :], xc[:, t, :], 0.0, ALU.mult, ALU.add))
                    own.settle()
                    dve.wait_ge(sem["gelued"], t + 1)
                    dve.tensor_tensor(tmp[:, 1, :], ii[:, t, :], gr[:, t, :], ALU.mult).then_inc(sem["y_ready"], 1)
                    dve.wait_ge(sem["y_high"], t + 1)
                    dve.tensor_tensor(mem.hl[:, 4 + t, :], tmp[:, 1, :], mem.hh[:, 4 + t, :].bitcast(F32),
                                      ALU.subtract).then_inc(sem["y_low"], 1)

                for c in range(A_Q, A_V):
                    split_low(dve, mem, sem, c + 1)
                    for t in range(2):
                        rotate(dve, own, mem, sem, A_TILE[c] + t, qk[:, 2 * (c - A_Q) + t, :], cos, sin)
                    if c == A_Q + 1:
                        for t in range(4):
                            gain(t)
                for c in (A_V, A_V + 1):
                    if c == A_V:
                        split_low(dve, mem, sem, c + 1)
                        own.settle()
                    for i in range(QT):
                        tile = A_TILE[c] + i
                        dve.wait_ge(sem["product"], tile + 1)
                        dve.tensor_scalar(v[:, i, (c - A_V) * CW:(c - A_V + 1) * CW], ps[:, tile % 4, 0:CW],
                                          small[:, QT + i:QT + i + 1], None, ALU.mult).then_inc(sem["drained"], 1)
                    for t in range(2):
                        recur(2 * (c - A_V) + t)

                def maxima(s):
                    n, b = P * (s % QT + 1), s % 2
                    dve.wait_ge(sem["scored"], s + 1)
                    own.mark(dve.tensor_reduce(small[:, SM_MAX + 2 * b:SM_MAX + 2 * b + 2], ps[:, 2 * b:2 * b + 2, 0:n], AX.X, ALU.max))
                    own.settle()
                    dve.tensor_scalar(small[:, SM_NEG + 2 * b:SM_NEG + 2 * b + 2], small[:, SM_MAX + 2 * b:SM_MAX + 2 * b + 2],
                                      -(DH ** -0.5), None, ALU.mult).then_inc(sem["maxed"], 1)

                def mix(s):
                    n, b = P * (s % QT + 1), s % 2
                    inv = small[:, SM_INV + 2 * b:SM_INV + 2 * b + 2]
                    dve.wait_ge(sem["exped"], 2 * (s + 1))
                    own.mark(dve.reciprocal(inv, small[:, SM_SUM + 2 * b:SM_SUM + 2 * b + 2]))
                    own.settle()
                    own.mark(dve.tensor_tensor(inv[:, 1:2], inv[:, 1:2], nlam, ALU.mult))
                    if s >= 2:
                        dve.wait_ge(sem["turned"], s - 1)
                    own.mark(dve.tensor_scalar(mixed[:, b, 0:n], prob[:, b, 0, 0:n], inv[:, 0:1], None, ALU.mult))
                    own.settle()
                    dve.scalar_tensor_tensor(out=mixed[:, b, 0:n], in0=prob[:, b, 1, 0:n], scalar=inv[:, 1:2],
                                             in1=mixed[:, b, 0:n], op0=ALU.mult, op1=ALU.add).then_inc(sem["mixed_done"], 1)

                def head_mean(h):
                    dve.wait_ge(sem["o_summed"], h + 1)
                    dve.tensor_scalar(small[:, SM_OMS:SM_OMS + QT], ps[:, 4, 8:8 + QT], 1.0 / P, EPS, ALU.mult, ALU.add)\
                        .then_inc(sem["o_mean"], 1)
                    dve.wait_ge(sem["o_root"], h + 1)
                    if h:
                        dve.wait_ge(sem["o_spread"], h)
                    diagonals(dve, mem, small[:, SM_ORS:SM_ORS + QT]).then_inc(sem["o_diag"], 1)

                def head_norm(h):
                    dve.wait_ge(sem["o_spread"], h + 1)
                    dve.wait_ge(sem["copied"], h + 1)
                    dve.scalar_tensor_tensor(out=tmp[:, 1, :], in0=head_out[:, h % 2, :], scalar=gsub, in1=ps[:, 7, :],
                                             op0=ALU.mult, op1=ALU.mult).then_inc(sem["o_ready"], 1)
                    dve.wait_ge(sem["o_high"], h + 1)
                    dve.tensor_tensor(mem.hl[:, h, :], tmp[:, 1, :], mem.hh[:, h, :].bitcast(F32),
                                      ALU.subtract).then_inc(sem["o_low"], 1)

                maxima(0)
                for s in range(STEPS):
                    if s + 1 < STEPS:
                        maxima(s + 1)
                    mix(s)
                    h, i = divmod(s, QT)
                    if h and i == 1:
                        head_mean(h - 1)
                    if h and i == 2:
                        head_norm(h - 1)
                    if s == 9:
                        split_low(dve, mem, sem, A_OUT)
                        split_low(dve, mem, sem, A_OUT + 1)
                head_mean(HEADS1 - 1)
                head_norm(HEADS1 - 1)

                def add_to_x(tile, k, per=once):
                    dve.wait_ge(sem["product"], tile + 1 + per(4 * BC))
                    dve.tensor_tensor(x[:, k, :], x[:, k, :], ps[:, tile % 4, :], ALU.add).then_inc(sem["drained"], 1)

                for c in range(A_OUT, A_PROJ):
                    if c + 1 >= A_OUT + 2:
                        split_low(dve, mem, sem, c + 1)
                    for t in range(2):
                        k = 2 * (c - A_OUT) + t
                        add_to_x(A_TILE[c] + t, k)
                        gain_low(dve, mem, sem, 1, k, AP_GMLP)
                    if c == A_OUT:
                        dve.wait_ge(sem["embed_high"], 1)
                        dve.tensor_tensor(mem.pl[:, :, :], mem.praw[:, :, :], mem.ph[:, :, :].bitcast(F32),
                                          ALU.subtract).then_inc(sem["embed_low"], 1)
                for t in range(KT):
                    tile = A_TILE[A_PROJ] + t
                    dve.wait_ge(sem["product"], tile + 1)
                    dve.tensor_copy(proj[:, t, :], ps[:, tile % 4, :]).then_inc(sem["drained"], 1)
                    if t == 0:
                        mean_square(dve, mem, sem, 1)
                        root_diagonals(dve, mem, sem, 1)
                        split_low(dve, mem, sem, A_MLP)
                dve.wait_ge(sem["kept"], 2)

                def mlp_first(c0, per, j):
                    for i in range(BC):
                        split_low(dve, mem, sem, c0 + i + 1, per)
                        for t in range(2):
                            tile = A_TILE[c0 + i] + t
                            dve.wait_ge(sem["product"], tile + 1 + per(4 * BC))
                            dve.tensor_tensor(tmp[:, 0, :], ps[:, tile % 4, :], mem.rb[:, :], ALU.mult).then_inc(sem["drained"], 1)
                            dve.wait_ge(sem["drained"], tile + 1 + per(4 * BC))
                            dve.scalar_tensor_tensor(out=tmp[:, 1, :], in0=tmp[:, 0, :], scalar=0.0, in1=tmp[:, 0, :],
                                                     op0=ALU.max, op1=ALU.mult).then_inc(sem["hidden"], 1)
                            dve.wait_ge(sem["hidden_high"], 2 * i + t + 1 + j * KT)
                            dve.tensor_tensor(mem.hl[:, 2 * i + t, :], tmp[:, 1, :], mem.hh[:, 2 * i + t, :].bitcast(F32),
                                              ALU.subtract).then_inc(sem["hidden_low"], 1)

                with dve.Fori(0, FB - 1) as j:
                    def per(n):
                        return j * n

                    mlp_first(A_MLP, per, j)
                    for i in range(BC, 2 * BC):
                        split_low(dve, mem, sem, A_MLP + i + 1, per)
                        for t in range(2):
                            add_to_x(A_TILE[A_MLP + i] + t, 2 * (i - BC) + t, per)
                c0 = A_GATE - 2 * BC
                mlp_first(c0, once, FB - 1)
                for c in range(c0 + BC, A_GATE):
                    split_low(dve, mem, sem, c + 1)
                    for t in range(2):
                        k = 2 * (c - c0 - BC) + t
                        add_to_x(A_TILE[c] + t, k)
                        gain_low(dve, mem, sem, 2, k, AP_GPLE)
                mean_square(dve, mem, sem, 2)
                root_diagonals(dve, mem, sem, 2)
                dve.wait_ge(sem["kept"], 3)
                for c in range(A_GATE, A_CHUNKS):
                    if c + 1 < A_CHUNKS:
                        split_low(dve, mem, sem, c + 1)
                    for t in range(2):
                        n = 2 * (c - A_GATE) + t
                        drain(tmp[:, 0, :], A_TILE[c] + t)
                        dve.wait_ge(sem["gate_out"], n + 1)
                        own.mark(dve.tensor_tensor(tmp[:, 1, :], tmp[:, 1, :], proj[:, n, :], ALU.mult))
                        own.settle()
                        own.mark(dve.tensor_tensor(x[:, n, :], x[:, n, :], tmp[:, 1, :], ALU.add))

            @block.tensor
            def _(pe):
                for k in range(KT):
                    sum_slice(pe, mem, sem, 0, k)

                def gained(n):
                    return lambda k: pe.wait_ge(sem["gain_low"], KT * n + k + 1)

                def linear_chunk(c, high, low, before=None, order=range(KT), after=None, per=once):
                    for t in range(2):
                        tile = A_TILE[c] + t
                        product_tile(pe, mem, sem, c, P * t, tile, high, low, order, before if t == 0 else None, per=per)
                        if after:
                            after(tile)

                linear_chunk(0, mem.gh, mem.gl, gained(0), after=lambda tile: spread_root(pe, mem, sem, 0) if tile == 0 else None)
                for c in (1, 2):
                    linear_chunk(c, mem.gh, mem.gl)
                pe.wait_ge(sem["positioned"], 32)
                for t in range(4):
                    pe.wait_ge(sem["conv"], t + 1)
                    for g in range(2):
                        if t:
                            pe.wait_ge(sem["gated"], 2 * t - 1 + g)
                        pe.matmul(ps[:, 6 + g, :], gw[:, g, t, :], xc[:, t, :], start=True, stop=True).then_inc(sem["gate_product"], 1)
                for c in range(3, A_V):
                    linear_chunk(c, mem.gh, mem.gl)
                for c in (A_V, A_V + 1):
                    for i in range(QT):
                        token_tile(pe, mem, sem, c, i, A_TILE[c] + i)

                def scores(s):
                    h, i = divmod(s, QT)
                    n, b = P * (i + 1), s % 2
                    if s >= 2:
                        pe.wait_ge(sem["exped"], 2 * (s - 1))
                    for c in range(2):
                        half = slice(DH * c, DH * (c + 1))
                        out = ps[:, 2 * b + c, 0:n]
                        pe.matmul(out, qk[half, h, P * i:n], qk[half, 4 + h, 0:n], start=True, stop=False, skip_group_check=True)
                        last = pe.matmul(out[:, n - P:n], ident, cst[:, C_TRI:C_TRI + P], start=False, stop=True, skip_group_check=True)
                    last.then_inc(sem["scored"], 1)

                def turn(s):
                    h, i = divmod(s, QT)
                    pe.wait_ge(sem["mixed_done"], s + 1)
                    if s:
                        pe.wait_ge(sem["untangled"], s)
                    for k in range(i + 1):
                        last = pe.transpose(ps[:, 5, P * k:P * (k + 1)], mixed[:, s % 2, P * k:P * (k + 1)], ident)
                    last.then_inc(sem["turned"], 1)

                def weigh(h):
                    pe.wait_ge(sem["untangled"], QT * (h + 1))
                    if h:
                        pe.wait_ge(sem["o_squared"], h)
                    for k in range(QT):
                        last = pe.matmul(ps[:, 6, P * k:S], v[:, k, P * h:P * (h + 1)], pt[:, h % 2, k, P * k:S],
                                         start=(k == 0), stop=(k == QT - 1), skip_group_check=True)
                    last.then_inc(sem["weighted"], 1)

                def head_sums(h):
                    pe.wait_ge(sem["o_squared"], h + 1)
                    if h:
                        pe.wait_ge(sem["o_mean"], h)
                    for i in range(QT):
                        last = pe.matmul(ps[:, 4, 8 + i:9 + i], mem.sq[:, h % 2, P * i:P * (i + 1)], ones[:, 0:1],
                                         start=(i == 0), stop=True, skip_group_check=True)
                    last.then_inc(sem["o_summed"], 1)

                def head_spread(h):
                    pe.wait_ge(sem["o_diag"], h + 1)
                    if h:
                        pe.wait_ge(sem["o_ready"], h)
                    pe.matmul(ps[:, 7, :], ones, tmp[:, 3, :], start=True, stop=True).then_inc(sem["o_spread"], 1)

                pe.wait_ge(sem["drained"], A_TILE[A_OUT])
                scores(0)
                for s in range(STEPS):
                    if s + 1 < STEPS:
                        scores(s + 1)
                    h, i = divmod(s, QT)
                    if h and i == 0:
                        weigh(h - 1)
                    if h and i == 1:
                        head_sums(h - 1)
                    turn(s)
                    if h and i == 2:
                        head_spread(h - 1)
                weigh(HEADS1 - 1)
                head_sums(HEADS1 - 1)
                head_spread(HEADS1 - 1)

                def mixer_ready(k):
                    if k >= 4:
                        pe.wait_ge(sem["y_low"], k - 3)
                    else:
                        pe.wait_ge(sem["o_low"], k + 1)

                for c in range(A_OUT, A_PROJ):
                    linear_chunk(c, mem.hh, mem.hl, mixer_ready if c == A_OUT else None, (4, 5, 6, 7, 0, 1, 2, 3),
                                 lambda tile: sum_slice(pe, mem, sem, 1, tile - 25) if tile > 24 else None)
                pe.wait_ge(sem["embed_low"], 1)
                pe.wait_ge(sem["low"], A_PROJ + 1)
                for t in range(KT):
                    tile = A_TILE[A_PROJ] + t
                    pe.wait_ge(sem["drained"], tile - 3)
                    for k in range(2):
                        at = D * k + P * t
                        last = three_passes(pe, ps[:, tile % 4, :], mem.wh[:, A_PROJ % 2, at:at + P], mem.wl[:, A_PROJ % 2, at:at + P],
                                            mem.ph[:, k, :], mem.pl[:, k, :], k == 0, k == 1)
                    last.then_inc(sem["product"], 1)
                    if t == 0:
                        sum_slice(pe, mem, sem, 1, KT - 1)
                    if t == 4:
                        spread_root(pe, mem, sem, 1)

                def mlp(c0, per, j, after=None):
                    for i in range(BC):
                        linear_chunk(c0 + i, mem.gh, mem.gl, gained(1) if i == 0 else None, per=per)
                    for i in range(BC, 2 * BC):
                        linear_chunk(c0 + i, mem.hh, mem.hl,
                                     (lambda k: pe.wait_ge(sem["hidden_low"], k + 1 + j * KT)) if i == BC else None, after=after, per=per)

                with pe.Fori(0, FB - 1) as j:
                    mlp(A_MLP, lambda n: j * n, j)
                c0 = A_GATE - 2 * BC
                first = A_TILE[c0 + BC]
                mlp(c0, once, FB - 1, lambda tile: sum_slice(pe, mem, sem, 2, tile - first - 1) if tile > first else None)

                def after_gate(tile):
                    if tile == A_TILE[A_GATE]:
                        sum_slice(pe, mem, sem, 2, KT - 1)
                    if tile == A_TILE[A_GATE] + 1:
                        spread_root(pe, mem, sem, 2)

                for c in range(A_GATE, A_CHUNKS):
                    linear_chunk(c, mem.gh, mem.gl, gained(2) if c == A_GATE else None, after=after_gate)
        clear(nc, used)



B_TILE = {c: 2 * c for c in range(B_V)}
B_TILE.update({B_V: 18, B_V + 1: 22})
B_TILE.update({c: 26 + 2 * (c - B_OUT) for c in range(B_OUT, B_CHUNKS + 1)})

B2_QK, B2_V, B2_CR, B2_U, B2_IQ, B2_IK, B2_SC, B2_MB = 0, 4096, 6144, 7168, 9280, 11328, 11840, 13376
B2_SUM = B2_QK + 4 * S
SB_IW, SB_TOP = 80, 112


def b_used(c):
    return B_TILE[c - 1]


def second_stack_layer(nc, mem, layer, weights, params, positions):
    ar, ps, cst, par, small, tmp, x = mem.arena, mem.ps, mem.cst, mem.par, mem.small, mem.tmp, mem.x
    qk = ar[:, B2_QK:B2_QK + 4096].rearrange("p (t s) -> p t s", s=S)
    branch = qk
    v = ar[:, B2_V:B2_V + 2048].rearrange("p (t s) -> p t s", s=S)
    cos, sin = ar[:, B2_CR:B2_CR + S], ar[:, B2_CR + S:B2_CR + 2 * S]
    W = PAD + S
    u = ar[:, B2_U:B2_U + 4 * W].rearrange("p (g s) -> p g s", s=W)
    window = [ar[:, B2_SUM + n * W:B2_SUM + (n + 1) * W] for n in range(2)]
    pooled = ar[:, B2_SUM + 2 * W:B2_SUM + 2 * W + S]
    iq = ar[:, B2_IQ:B2_IQ + 2048].rearrange("p (t s) -> p t s", s=S)
    ik = ar[:, B2_IK:B2_IK + S]
    score = ar[:, B2_SC:B2_SC + 3 * S].rearrange("p (i s) -> p i s", s=S)
    mask = ar[:, B2_MB:B2_MB + 1024].bitcast(BF16).rearrange("p (i s) -> p i s", s=S)
    prob = ar[:, B2_IK:B2_IK + 1024].rearrange("p (b s) -> p b s", b=2)
    scaled = ar[:, B2_IK + 1024:B2_IK + 2048].rearrange("p (b s) -> p b s", b=2)
    pt = [ar[:, a:a + 2048].rearrange("p (k s) -> p k s", s=S) for a in (B2_IQ, B2_U)]
    weight_rows = small[:, SB_IW:SB_IW + 32].rearrange("p (i h) -> p i h", h=HEADS2)
    top = small[:, SB_TOP:SB_TOP + 24].rearrange("p (i e) -> p i e", e=8)
    wpool = par[:, BP_WPOOL:BP_WPOOL + 4 * P].rearrange("p (g n) -> p g n", g=4)
    ident = cst[:, C_ID:C_ID + P]
    STEPS = QT * HEADS2
    LOGITS = [(i, h) for i in range(1, QT) for h in range(HEADS2)]

    with ExitStack() as ctx:
        sem, used = semaphores(nc, ctx, (
            "loaded0 loaded1 vectors positioned high low product drained squared summed mean root diag spread kept gain_high "
            "gain_low own tables turned_tables logit rectified weighed windowed pooled_ready pool_product pool_high pool_low "
            "scored maxed exped scaled_done turned untangled weighted pair_high pair_low updated zeroed hidden hidden_high "
            "hidden_low padded pool_own"))
        with nc.Block() as block:

            @block.sync
            def _(sp):
                def chunk(c, per=once, j=None):
                    row = (layer * B_CHUNKS + c) * P if j is None else (layer * B_CHUNKS + c + j * (2 * BC)) * P
                    load_chunk(sp, mem, sem, weights, row, c, per)

                rows = sp.snap(layer * P)
                sp.dma_start(par[:, 0:BP_N], params[bass.ds(rows, P), :]).then_inc(sem["vectors"], 16)
                sp.dma_start(tmp[:, 0, :].bitcast(I32), positions).then_inc(sem["positioned"], 16)
                for c in range(B_FF):
                    chunk(c)
                with sp.Fori(0, FB) as j:
                    for i in range(2 * BC):
                        chunk(B_FF + i, lambda n: j * n, j)

            @block.gpsimd
            def _(pool):
                own = Steps(pool, sem["pool_own"])
                pool.memset(u[:, :, 0:PAD], 0.0).then_inc(sem["padded"], 1)
                one_over_root(pool, mem, sem, 0)
                for g in range(4):
                    pool.wait_ge(sem["drained"], B_TILE[B_U] + g + 1)
                    pool.wait_ge(sem["padded"], 1)
                    if g:
                        pool.wait_ge(sem["pooled_ready"], g)
                    source, reach = u[:, g, :], 1
                    for n in range(g + 1):
                        own.settle() if own.count else None
                        last = pool.tensor_tensor(window[n % 2][:, 2 * reach - 1:W], source[:, 2 * reach - 1:W],
                                                  source[:, reach - 1:W - reach], ALU.add)
                        if n < g:
                            own.mark(last)
                        source, reach = window[n % 2], 2 * reach
                    last.then_inc(sem["windowed"], 1)
                one_over_root(pool, mem, sem, 1)
                pool.wait_ge(sem["updated"], KT)
                pool.memset(branch[:, :, :], 0.0).then_inc(sem["zeroed"], 1)
                one_over_root(pool, mem, sem, 2)
                one_over_root(pool, mem, sem, 3)

            @block.scalar
            def _(act):
                act.wait_ge(sem["vectors"], 16)
                for k in range(KT):
                    square_slice(act, mem, sem, 0, k, x)
                    gain_high(act, mem, sem, k, BP_GPRE)
                split_high(act, mem, sem, 0, 0)
                split_high(act, mem, sem, 1, 0)
                act.wait_ge(sem["tables"], 1)
                act.activation(sin, tmp[:, 1, :], ACT.Sin, scale=cst[:, C_SIGN:C_SIGN + 1]).then_inc(sem["turned_tables"], 1)
                act.activation(cos, tmp[:, 0, :], ACT.Sin, scale=-1.0, bias=cst[:, C_HPI:C_HPI + 1]).then_inc(sem["turned_tables"], 1)
                keep_root(act, mem, sem, 0)
                for c in range(2, 5):
                    split_high(act, mem, sem, c, b_used(c))
                for s, (i, h) in enumerate(LOGITS):
                    n = P * (i + 1)
                    act.wait_ge(sem["logit"], s + 1)
                    if s >= 2:
                        act.wait_ge(sem["weighed"], s - 1)
                    act.activation(tmp[:, s % 2, 0:n], ps[:, 6 + s % 2, 0:n], ACT.Relu, scale=DH ** -0.5).then_inc(sem["rectified"], 1)
                for c in range(5, 9):
                    split_high(act, mem, sem, c, b_used(c))
                    if c >= 7:
                        for g in range(2 * (c - 7), 2 * (c - 7) + 2):
                            act.wait_ge(sem["pool_product"], g + 1)
                            act.activation(mem.hh[:, g, :], ps[:, 6 + g % 2, :], ACT.Copy,
                                           scale=par[:, BP_SCALE + g:BP_SCALE + g + 1]).then_inc(sem["pool_high"], 1)
                for c in range(9, B_OUT + 1):
                    split_high(act, mem, sem, c, b_used(c))

                def exponents(s):
                    n, b = P * (s % QT + 1), s % 2
                    act.wait_ge(sem["maxed"], s + 1)
                    if s >= 2:
                        act.wait_ge(sem["scaled_done"], s - 1)
                    act.activation(prob[:, b, 0:n], ps[:, b, 0:n], ACT.Exp, scale=DH ** -0.5, bias=small[:, SM_NEG + b:SM_NEG + b + 1],
                                   accum_out=small[:, SM_SUM + b:SM_SUM + b + 1]).then_inc(sem["exped"], 1)

                def untangle(s):
                    h, i = divmod(s, QT)
                    act.wait_ge(sem["turned"], s + 1)
                    if h >= 2:
                        act.wait_ge(sem["weighted"], h - 1)
                    act.activation(pt[h % 2][:, 0:i + 1, P * i:P * (i + 1)],
                                   ps[:, 2 + s % 2, 0:P * (i + 1)].rearrange("p (k q) -> p k q", q=P), ACT.Copy).then_inc(sem["untangled"], 1)

                def pair_high(j):
                    act.wait_ge(sem["weighted"], 2 * j + 2)
                    act.activation(mem.hh[:, 4 + j, :], ps[:, 6 + j % 2, :], ACT.Copy).then_inc(sem["pair_high"], 1)

                exponents(0)
                for s in range(STEPS):
                    if s + 1 < STEPS:
                        exponents(s + 1)
                    untangle(s)
                    if s >= 8 and s % 8 == 2:
                        pair_high(s // 8 - 1)
                    if s == 4:
                        split_high(act, mem, sem, B_OUT + 1, b_used(B_OUT + 1))
                pair_high(3)
                for c in range(B_OUT, B_FF):
                    if B_OUT + 2 <= c + 1:
                        split_high(act, mem, sem, c + 1, b_used(c + 1))
                    for t in range(2):
                        act.wait_ge(sem["drained"], B_TILE[c] + t + 1)
                        square_slice(act, mem, sem, 1, 2 * (c - B_OUT) + t, branch)
                keep_root(act, mem, sem, 1)
                for k in range(KT):
                    act.wait_ge(sem["updated"], k + 1)
                    square_slice(act, mem, sem, 2, k, x)
                    gain_high(act, mem, sem, k, BP_FPRE)
                keep_root(act, mem, sem, 2)

                def mlp_first(c0, per, j):
                    for i in range(BC):
                        split_high(act, mem, sem, c0 + i + 1, b_used(c0 + i + 1), per)
                        for t in range(2):
                            act.wait_ge(sem["hidden"], 2 * i + t + 1 + j * KT)
                            act.activation(mem.hh[:, 2 * i + t, :], tmp[:, 1, :], ACT.Copy).then_inc(sem["hidden_high"], 1)

                with act.Fori(0, FB - 1) as j:
                    def per(n):
                        return j * n

                    mlp_first(B_FF, per, j)
                    for i in range(BC, 2 * BC):
                        split_high(act, mem, sem, B_FF + i + 1, b_used(B_FF + i + 1), per)
                c0 = B_CHUNKS - 2 * BC
                mlp_first(c0, once, FB - 1)
                for c in range(c0 + BC, B_CHUNKS):
                    if c + 1 < B_CHUNKS:
                        split_high(act, mem, sem, c + 1, b_used(c + 1))
                    for t in range(2):
                        act.wait_ge(sem["drained"], B_TILE[c] + t + 1)
                        square_slice(act, mem, sem, 3, 2 * (c - c0 - BC) + t, branch)
                keep_root(act, mem, sem, 3)

            @block.vector
            def _(dve):
                own = Steps(dve, sem['own'])
                dve.wait_ge(sem["positioned"], 16)
                rotary_angles(dve, own, mem, tmp[:, 0, :], tmp[:, 1, :]).then_inc(sem["tables"], 1)
                own.mark(dve.tensor_copy(mask[:, 0, 0:P], cst[:, C_CHUNK:C_CHUNK + P]))
                dve.wait_ge(sem["vectors"], 16)
                for k in range(KT):
                    gain_low(dve, mem, sem, 0, k, BP_GPRE)
                split_low(dve, mem, sem, 0)
                mean_square(dve, mem, sem, 0)
                root_diagonals(dve, mem, sem, 0)
                split_low(dve, mem, sem, 1)
                dve.wait_ge(sem["kept"], 1)
                dve.wait_ge(sem["turned_tables"], 2)
                own.mark(dve.tensor_tensor(sin, sin, mem.rb[:, :], ALU.mult))
                own.mark(dve.tensor_tensor(cos, cos, mem.rb[:, :], ALU.mult))
                own.settle()
                for t in range(4):
                    if t == 2:
                        split_low(dve, mem, sem, 2)
                    rotate(dve, own, mem, sem, t, iq[:, t, :], cos, sin)
                split_low(dve, mem, sem, 3)
                rotate(dve, own, mem, sem, 4, ik, cos, sin)
                dve.wait_ge(sem["product"], 6)
                for i in range(QT):
                    last = dve.tensor_scalar(weight_rows[:, i, :], ps[:, 5 % 4, 8 * i:8 * i + 8], small[:, QT + i:QT + i + 1],
                                             HEADS2 ** -0.5, ALU.mult, ALU.mult)
                    if i < QT - 1:
                        own.mark(last)
                own.settle()
                last.then_inc(sem["drained"], 1)

                def drain_u(c):
                    for t in range(2):
                        tile = B_TILE[c] + t
                        dve.wait_ge(sem["product"], tile + 1)
                        dve.tensor_tensor(u[:, tile - B_TILE[B_U], PAD:W], ps[:, tile % 4, :], mem.rb[:, :], ALU.mult)\
                            .then_inc(sem["drained"], 1)

                split_low(dve, mem, sem, 4)
                dve.wait_ge(sem["padded"], 1)
                drain_u(B_U)
                dve.wait_ge(sem["drained"], B_TILE[B_U])
                for s, (i, h) in enumerate(LOGITS):
                    n = P * (i + 1)
                    dve.wait_ge(sem["rectified"], s + 1)
                    out, scale = score[:, i - 1, 0:n], weight_rows[:, i, h:h + 1]
                    if h == 0:
                        dve.tensor_scalar(out, tmp[:, s % 2, 0:n], scale, None, ALU.mult).then_inc(sem["weighed"], 1)
                    else:
                        dve.wait_ge(sem["weighed"], s)
                        dve.scalar_tensor_tensor(out=out, in0=tmp[:, s % 2, 0:n], scalar=scale, in1=out,
                                                 op0=ALU.mult, op1=ALU.add).then_inc(sem["weighed"], 1)
                dve.wait_ge(sem["weighed"], len(LOGITS))
                for i in range(1, QT):
                    edge = score[:, i - 1, P * i:P * (i + 1)]
                    own.mark(dve.tensor_tensor(edge, edge, cst[:, C_CHUNK:C_CHUNK + P], ALU.add))

                def pick():
                    own.settle()
                    for i in range(1, QT):
                        own.mark(dve.max(top[:, i - 1, :], score[:, i - 1, 0:P * (i + 1)]))
                    found = own.count
                    for i in range(1, QT):
                        values = score[:, i - 1, 0:P * (i + 1)]
                        dve.wait_ge(sem["own"], found - (QT - 1 - i))
                        own.mark(dve.match_replace(out=values, in_to_replace=top[:, i - 1, :], in_values=values, imm_value=MARK))

                rounds = [0]

                def picks(n):
                    for _ in range(n):
                        pick()
                        rounds[0] += 1

                split_low(dve, mem, sem, 5)
                drain_u(B_U + 1)
                picks(2)

                def pool_values(g):
                    w = WINDOWS[g]
                    total = window[g % 2][:, PAD:W]
                    dve.wait_ge(sem["windowed"], g + 1)
                    if g:
                        dve.wait_ge(sem["pool_product"], g)
                    own.settle()
                    own.mark(dve.scalar_tensor_tensor(out=pooled, in0=total, scalar=1.0 / w, in1=u[:, g, PAD:W],
                                                      op0=ALU.mult, op1=ALU.subtract))
                    own.settle()
                    own.mark(dve.tensor_tensor(pooled[:, 0:PAD], total[:, 0:PAD], cst[:, C_CNT + PAD * g:C_CNT + PAD * (g + 1)], ALU.mult))
                    own.settle()
                    dve.tensor_tensor(pooled[:, 0:PAD], pooled[:, 0:PAD], u[:, g, PAD:2 * PAD], ALU.subtract).then_inc(sem["pooled_ready"], 1)

                def pool_low(g):
                    dve.wait_ge(sem["pool_high"], g + 1)
                    dve.scalar_tensor_tensor(out=mem.hl[:, g, :], in0=ps[:, 6 + g % 2, :], scalar=par[:, BP_SCALE + g:BP_SCALE + g + 1],
                                             in1=mem.hh[:, g, :].bitcast(F32), op0=ALU.mult, op1=ALU.subtract).then_inc(sem["pool_low"], 1)

                for c in range(B_Q, B_V):
                    split_low(dve, mem, sem, c + 1)
                    for t in range(2):
                        if c == B_K and t == 0:
                            dve.wait_ge(sem["pool_product"], 4)
                        rotate(dve, own, mem, sem, B_TILE[c] + t, qk[:, 2 * (c - B_Q) + t, :], cos, sin)
                        if c == B_Q:
                            pool_values(t)
                        if c == B_Q + 1:
                            pool_low(t)
                            pool_values(2 + t)
                        if c == B_K:
                            pool_low(2 + t)
                        picks(1)
                for c in (B_V, B_V + 1):
                    if c == B_V:
                        split_low(dve, mem, sem, c + 1)
                        own.settle()
                    for i in range(QT):
                        tile = B_TILE[c] + i
                        dve.wait_ge(sem["product"], tile + 1)
                        dve.tensor_scalar(v[:, i, (c - B_V) * CW:(c - B_V + 1) * CW], ps[:, tile % 4, 0:CW],
                                          small[:, QT + i:QT + i + 1], None, ALU.mult).then_inc(sem["drained"], 1)
                        if i % 2:
                            picks(1)
                picks(TOPK // 8 - rounds[0])
                own.settle()
                for i in range(1, QT):
                    n = P * (i + 1)
                    own.mark(dve.tensor_scalar(mask[:, i, 0:n], score[:, i - 1, 0:n], 0.9 * MARK, NEG, ALU.is_gt, ALU.mult))
                own.settle()
                split_low(dve, mem, sem, B_OUT)

                def maxima(s):
                    n, b = P * (s % QT + 1), s % 2
                    dve.wait_ge(sem["scored"], s + 1)
                    own.mark(dve.tensor_reduce(small[:, SM_MAX + b:SM_MAX + b + 1], ps[:, b, 0:n], AX.X, ALU.max))
                    own.settle()
                    dve.tensor_scalar(small[:, SM_NEG + b:SM_NEG + b + 1], small[:, SM_MAX + b:SM_MAX + b + 1],
                                      -(DH ** -0.5), None, ALU.mult).then_inc(sem["maxed"], 1)

                def scale_rows(s):
                    n, b = P * (s % QT + 1), s % 2
                    inv = small[:, SM_INV + b:SM_INV + b + 1]
                    dve.wait_ge(sem["exped"], s + 1)
                    own.mark(dve.reciprocal(inv, small[:, SM_SUM + b:SM_SUM + b + 1]))
                    own.settle()
                    if s >= 2:
                        dve.wait_ge(sem["turned"], s - 1)
                    dve.tensor_scalar(scaled[:, b, 0:n], prob[:, b, 0:n], inv, None, ALU.mult).then_inc(sem["scaled_done"], 1)

                def pair_low(j):
                    dve.wait_ge(sem["pair_high"], j + 1)
                    dve.tensor_tensor(mem.hl[:, 4 + j, :], ps[:, 6 + j % 2, :], mem.hh[:, 4 + j, :].bitcast(F32),
                                      ALU.subtract).then_inc(sem["pair_low"], 1)

                maxima(0)
                for s in range(STEPS):
                    if s + 1 < STEPS:
                        maxima(s + 1)
                    scale_rows(s)
                    if s >= 8 and s % 8 == 3:
                        pair_low(s // 8 - 1)
                    if s == 5:
                        split_low(dve, mem, sem, B_OUT + 1)
                pair_low(3)
                for c in range(B_OUT, B_FF):
                    if B_OUT + 2 <= c + 1:
                        split_low(dve, mem, sem, c + 1)
                    for t in range(2):
                        tile = B_TILE[c] + t
                        dve.wait_ge(sem["product"], tile + 1)
                        dve.tensor_copy(branch[:, 2 * (c - B_OUT) + t, :], ps[:, tile % 4, :]).then_inc(sem["drained"], 1)
                mean_square(dve, mem, sem, 1)
                root_diagonals(dve, mem, sem, 1)

                def add_branch(n, k, gains, signal):
                    own.settle()
                    own.mark(dve.scalar_tensor_tensor(out=tmp[:, k % 2, :], in0=branch[:, k, :], scalar=par[:, gains + k:gains + k + 1],
                                                      in1=mem.rb[:, :], op0=ALU.mult, op1=ALU.mult))
                    own.settle()
                    dve.tensor_tensor(x[:, k, :], x[:, k, :], tmp[:, k % 2, :], ALU.add).then_inc(signal, 1)

                dve.wait_ge(sem["kept"], 2)
                for k in range(KT):
                    add_branch(1, k, BP_GPOST, sem["updated"])
                    if k:
                        gain_low(dve, mem, sem, 1, k - 1, BP_FPRE)
                gain_low(dve, mem, sem, 1, KT - 1, BP_FPRE)
                mean_square(dve, mem, sem, 2)
                root_diagonals(dve, mem, sem, 2)
                dve.wait_ge(sem["kept"], 3)
                dve.wait_ge(sem["zeroed"], 1)

                def mlp_first(c0, per, j):
                    for i in range(BC):
                        split_low(dve, mem, sem, c0 + i + 1, per)
                        for t in range(2):
                            tile = B_TILE[c0 + i] + t
                            dve.wait_ge(sem["product"], tile + 1 + per(4 * BC))
                            dve.tensor_tensor(tmp[:, 0, :], ps[:, tile % 4, :], mem.rb[:, :], ALU.mult).then_inc(sem["drained"], 1)
                            dve.wait_ge(sem["drained"], tile + 1 + per(4 * BC))
                            dve.scalar_tensor_tensor(out=tmp[:, 1, :], in0=tmp[:, 0, :], scalar=0.0, in1=tmp[:, 0, :],
                                                     op0=ALU.max, op1=ALU.mult).then_inc(sem["hidden"], 1)
                            dve.wait_ge(sem["hidden_high"], 2 * i + t + 1 + j * KT)
                            dve.tensor_tensor(mem.hl[:, 2 * i + t, :], tmp[:, 1, :], mem.hh[:, 2 * i + t, :].bitcast(F32),
                                              ALU.subtract).then_inc(sem["hidden_low"], 1)

                def mlp_second(c0, per):
                    for i in range(BC, 2 * BC):
                        if c0 + i + 1 < B_CHUNKS:
                            split_low(dve, mem, sem, c0 + i + 1, per)
                        for t in range(2):
                            tile, k = B_TILE[c0 + i] + t, 2 * (i - BC) + t
                            dve.wait_ge(sem["product"], tile + 1 + per(4 * BC))
                            dve.tensor_tensor(branch[:, k, :], branch[:, k, :], ps[:, tile % 4, :], ALU.add).then_inc(sem["drained"], 1)

                with dve.Fori(0, FB - 1) as j:
                    def per(n):
                        return j * n

                    mlp_first(B_FF, per, j)
                    mlp_second(B_FF, per)
                mlp_first(B_CHUNKS - 2 * BC, once, FB - 1)
                mlp_second(B_CHUNKS - 2 * BC, once)
                mean_square(dve, mem, sem, 3)
                root_diagonals(dve, mem, sem, 3)
                dve.wait_ge(sem["kept"], 4)
                for k in range(KT):
                    add_branch(3, k, BP_FPOST, sem["updated"])

            @block.tensor
            def _(pe):
                def gained(n, also=None):
                    def before(k):
                        pe.wait_ge(sem["gain_low"], KT * (n // 2) + k + 1)
                        if also:
                            also(k)
                    return before

                def linear_chunk(c, high, low, before=None, order=range(KT), after=None, per=once):
                    for t in range(2):
                        tile = B_TILE[c] + t
                        product_tile(pe, mem, sem, c, P * t, tile, high, low, order, before if t == 0 else None, per=per)
                        if after:
                            after(tile)

                for k in range(KT):
                    sum_slice(pe, mem, sem, 0, k)
                linear_chunk(0, mem.gh, mem.gl, gained(0), after=lambda tile: spread_root(pe, mem, sem, 0) if tile == 0 else None)
                linear_chunk(1, mem.gh, mem.gl)
                product_tile(pe, mem, sem, B_IKW, 0, 4, mem.gh, mem.gl)
                pe.wait_ge(sem["drained"], 2)
                wh = mem.wh[:, B_IKW % 2, :].rearrange("p (k n) -> p k n", k=KT)
                wl = mem.wl[:, B_IKW % 2, :].rearrange("p (k n) -> p k n", k=KT)
                for i in range(QT):
                    for k in range(KT):
                        last = three_passes(pe, ps[:, 1, 8 * i:8 * i + 8], wh[:, k, P:P + 8], wl[:, k, P:P + 8],
                                            mem.gh[:, k, P * i:P * (i + 1)], mem.gl[:, k, P * i:P * (i + 1)],
                                            i == 0 and k == 0, i == QT - 1 and k == KT - 1, swap=True)
                last.then_inc(sem["product"], 1)
                linear_chunk(3, mem.gh, mem.gl)
                pe.wait_ge(sem["drained"], 6)
                for s, (i, h) in enumerate(LOGITS):
                    half = slice(DH * (h % 2), DH * (h % 2 + 1))
                    if s >= 2:
                        pe.wait_ge(sem["rectified"], s - 1)
                    pe.matmul(ps[:, 6 + s % 2, 0:P * (i + 1)], iq[half, h // 2, P * i:P * (i + 1)], ik[half, 0:P * (i + 1)],
                              start=True, stop=True).then_inc(sem["logit"], 1)
                linear_chunk(4, mem.gh, mem.gl)

                def pool_product(g):
                    pe.wait_ge(sem["pooled_ready"], g + 1)
                    pe.wait_ge(sem["rectified"], len(LOGITS))
                    if g >= 2:
                        pe.wait_ge(sem["pool_low"], g - 1)
                    pe.matmul(ps[:, 6 + g % 2, :], wpool[:, g, :], pooled, start=True, stop=True).then_inc(sem["pool_product"], 1)

                linear_chunk(5, mem.gh, mem.gl)
                linear_chunk(6, mem.gh, mem.gl, after=lambda tile: pool_product(tile - B_TILE[6]))
                pool_product(2)
                pool_product(3)
                for c in (7, 8):
                    linear_chunk(c, mem.gh, mem.gl)
                for c in (B_V, B_V + 1):
                    for i in range(QT):
                        token_tile(pe, mem, sem, c, i, B_TILE[c] + i)

                def scores(s):
                    h, i = divmod(s, QT)
                    n = P * (i + 1)
                    half = slice(DH * (h % 2), DH * (h % 2 + 1))
                    if s >= 2:
                        pe.wait_ge(sem["exped"], s - 1)
                    pe.matmul(ps[:, s % 2, 0:n], qk[half, h // 2, P * i:n], qk[half, 4 + h // 2, 0:n],
                              start=True, stop=False, skip_group_check=True)
                    pe.matmul(ps[:, s % 2, 0:n], mem.idb[:, :], mask[:, i, 0:n], start=False, stop=True,
                              skip_group_check=True).then_inc(sem["scored"], 1)

                def turn(s):
                    h, i = divmod(s, QT)
                    pe.wait_ge(sem["scaled_done"], s + 1)
                    if s >= 2:
                        pe.wait_ge(sem["untangled"], s - 1)
                    for k in range(i + 1):
                        last = pe.transpose(ps[:, 2 + s % 2, P * k:P * (k + 1)], scaled[:, s % 2, P * k:P * (k + 1)], ident)
                    last.then_inc(sem["turned"], 1)

                def weigh(h):
                    j = h // 2
                    pe.wait_ge(sem["untangled"], QT * (h + 1))
                    if h % 2 == 0 and j >= 2:
                        pe.wait_ge(sem["pair_low"], j - 1)
                    out = ps[DH * (h % 2):DH * (h % 2 + 1), 6 + j % 2, :]
                    for k in range(QT):
                        last = pe.matmul(out[:, P * k:S], v[:, k, DH * h:DH * (h + 1)], pt[h % 2][:, k, P * k:S],
                                         start=(k == 0), stop=(k == QT - 1), skip_group_check=True)
                    last.then_inc(sem["weighted"], 1)

                pe.wait_ge(sem["drained"], B_TILE[B_OUT])
                pe.wait_ge(sem["low"], B_OUT + 1)
                scores(0)
                for s in range(STEPS):
                    if s + 1 < STEPS:
                        scores(s + 1)
                    if s and s % QT == 0:
                        weigh(s // QT - 1)
                    turn(s)
                weigh(HEADS2 - 1)

                def mixer_ready(k):
                    if k < 4:
                        pe.wait_ge(sem["pool_low"], k + 1)
                    else:
                        pe.wait_ge(sem["pair_low"], k - 3)

                first = B_TILE[B_OUT]
                for c in range(B_OUT, B_FF):
                    linear_chunk(c, mem.hh, mem.hl, mixer_ready if c == B_OUT else None,
                                 after=lambda tile: sum_slice(pe, mem, sem, 1, tile - first - 1) if tile > first else None)
                sum_slice(pe, mem, sem, 1, KT - 1)
                spread_root(pe, mem, sem, 1)

                def mlp(c0, per, j, before, after_first=None, after_second=None):
                    for i in range(BC):
                        linear_chunk(c0 + i, mem.gh, mem.gl, before if i == 0 else None, after=after_first, per=per)
                    for i in range(BC, 2 * BC):
                        linear_chunk(c0 + i, mem.hh, mem.hl,
                                     (lambda k: pe.wait_ge(sem["hidden_low"], k + 1 + j * KT)) if i == BC else None, after=after_second, per=per)

                mlp(B_FF, once, 0, gained(2, lambda k: sum_slice(pe, mem, sem, 2, k)),
                    lambda tile: spread_root(pe, mem, sem, 2) if tile == B_TILE[B_FF] else None)
                with pe.Fori(1, FB - 1) as j:
                    mlp(B_FF, lambda n: j * n, j, None)
                c0 = B_CHUNKS - 2 * BC
                last_first = B_TILE[c0 + BC]
                mlp(c0, once, FB - 1, None,
                    after_second=lambda tile: sum_slice(pe, mem, sem, 3, tile - last_first - 1) if tile > last_first else None)
                sum_slice(pe, mem, sem, 3, KT - 1)
                spread_root(pe, mem, sem, 3)
        clear(nc, used)



def chunks(w):
    k, n = w.shape
    return w.reshape(k // P, P, n // CW, CW).transpose(2, 1, 0, 3).reshape(-1, k // P * CW)


def columns(v):
    return v.reshape(-1, P).T


def constant_table():
    t = np.zeros((P, C_N), np.float32)
    p = np.arange(P)
    t[:, C_ID:C_ID + P] = np.eye(P)
    t[:, C_ONES:C_ONES + P] = 1.0
    t[:, C_TRI:C_TRI + P] = np.where(p[:, None] >= p[None, :], 0.0, NEG)
    t[:, C_CHUNK:C_CHUNK + P] = np.where(p[:, None] // 64 >= p[None, :] // 64, 0.0, NEG)
    d = p % DH
    freq = np.float32(THETA) ** (-np.arange(ROT_HALF, dtype=np.float32) / ROT_HALF)
    t[:, C_FREQ] = np.where(d < 2 * ROT_HALF, freq[d % ROT_HALF], 0.0)
    t[:, C_SIGN] = np.where(d < ROT_HALF, -1.0, 1.0)
    for g, w in enumerate(WINDOWS):
        t[:, C_CNT + PAD * g:C_CNT + PAD * (g + 1)] = 1.0 / np.minimum(np.arange(PAD) + 1, w)
    t[:, C_HPI] = np.pi / 2
    t[:, C_MHALF:C_MHALF + QT] = -0.5
    return t


def launch_arrays(inp):
    f = {k: np.asarray(a) for k, a in inp.items()}
    wa, pa, gates, embed = [], [], [], []
    for l in range(DEPTH):
        w = f["w_in"][l]
        q, k, v, xr, gr = (w[:, a:b] for a, b in ((0, 512), (512, 1024), (1024, 1536), (1536, 2048), (2048, 2560)))
        wa += [chunks(m) for m in (xr, gr, q, k, v, f["w_out"][l])]
        wa += [f["w_ple_proj"][l].reshape(2, P, D).transpose(1, 0, 2).reshape(P, CHUNK)]
        for j in range(FB):
            wa += [chunks(f["w_mlp_in"][l][:, D * j:D * (j + 1)]), chunks(f["w_mlp_out"][l][D * j:D * (j + 1)])]
        wa += [chunks(f["w_ple_gate"][l])]
        wide = lambda a: np.broadcast_to(a.reshape(1, -1), (P, a.size))
        lam_init = 0.8 - 0.6 * math.exp(-0.3 * l)
        pa += [np.concatenate([
            columns(f["g_mix"][l]), columns(f["g_mlp"][l]), columns(f["g_ple"][l]), columns(f["g_subln"][l]),
            *[columns(f["conv_w"][l][t]) for t in range(CONV)], columns(f["conv_b"][l]),
            columns(f["b_gate_a"][l]), columns(f["b_gate_x"][l]), columns(f["lru_lambda"][l]),
            wide(f["lam_q"][l]), wide(f["lam_k"][l]),
            np.full((P, 1), lam_init, np.float32), np.full((P, 1), 1.0 - lam_init, np.float32)], axis=1)]
        g = np.zeros((2, 4, P, P), np.float32)
        for n, name in enumerate(("w_gate_a", "w_gate_x")):
            g[n, :, :64, :64] = f[name][l][0::2]
            g[n, :, 64:, 64:] = f[name][l][1::2]
        gates += [g.transpose(2, 0, 1, 3).reshape(P, -1)]
        embed += [f["p"][l, 0].T.reshape(2, P, S).transpose(1, 0, 2).reshape(P, -1)]
    wb, pb = [], []
    for l in range(DEPTH):
        w = f["w_in_2"][l]
        u, q, k, v, iq, ik, iw = np.split(w, np.cumsum((512, 512, 512, 512, 512, 64)), axis=1)
        ikw = np.zeros((D, CW), np.float32)
        ikw[:, 0:64], ikw[:, 64:128], ikw[:, 128:136] = ik, ik, iw
        wb += [chunks(m) for m in (iq, ikw, u, q, k, v, f["w_out_2"][l])]
        for j in range(FB):
            wb += [chunks(f["w_ff1_2"][l][:, D * j:D * (j + 1)]), chunks(f["w_ff2_2"][l][D * j:D * (j + 1)])]
        pb += [np.concatenate([
            columns(f["g_pre_mix_2"][l]), columns(f["g_post_mix_2"][l]), columns(f["g_pre_ffn_2"][l]),
            columns(f["g_post_ffn_2"][l]), columns(f["pool_scale_2"][l]),
            f["w_pool_2"][l].transpose(1, 0, 2).reshape(P, -1)], axis=1)]
    table = constant_table()
    table[:, C_GFIN:C_GFIN + KT] = columns(f["g_final"])
    spread = lambda a: np.broadcast_to(a.reshape(1, S), (P, S))
    out = {
        "weights_a": np.concatenate(wa), "weights_b": np.concatenate(wb), "params_a": np.concatenate(pa),
        "params_b": np.concatenate(pb), "gates": np.concatenate(gates), "embed": np.concatenate(embed),
        "constants": table, "positions": np.concatenate([spread(f["positions"]), spread(f["positions_2"])]),
        "xt": f["x"][0].T,
    }
    return {n: np.ascontiguousarray(a) for n, a in out.items()}


def kernel(**inputs):
    import concourse.bacc as bacc
    from concourse.bass_utils import run_bass_kernel_spmd

    nc = bacc.Bacc("TRN2", target_bir_lowering=False, num_devices=1)
    arrays = {f"in_{name}": a for name, a in launch_arrays(inputs).items()}
    args = [nc.dram_tensor(name, a.shape, mybir.dt.from_np(a.dtype), kind="ExternalInput").ap() for name, a in arrays.items()]
    args.append(nc.dram_tensor("out_yt", (D, S), F32, kind="ExternalOutput").ap())
    build(nc, *args)
    r = run_bass_kernel_spmd(nc, [arrays], core_ids=[0])
    return np.ascontiguousarray(r.results[0]["out_yt"].T).reshape(1, S, D)
```

```python
import math
from contextlib import ExitStack

import numpy as np

import concourse.bass as bass
from concourse import mybir

F32 = mybir.dt.float32
F32R = mybir.dt.float32r
BF16 = mybir.dt.bfloat16
I32 = mybir.dt.int32
ALU = mybir.AluOpType
ACT = mybir.ActivationFunctionType
AX = mybir.AxisListType

P = 128
D = 1024
S = 512
KT = D // P
QT = S // P
DEPTH = 2
EPS = 1e-6
CW = 256
CHUNK = KT * CW
D_FF = 4 * D
FB = D_FF // D
BC = D // CW
HEADS1 = 4
HEADS2 = 8
DH = 64
TOPK = 128
ROT_HALF = 8
THETA = 500000.0
NEG = -1.0e30
MARK = -3.0e38
WINDOWS = (2, 4, 8, 16)
PAD = 16
CONV = 4

A_XR, A_GR, A_Q, A_K, A_V = 0, 2, 4, 6, 8
A_OUT = 10
A_PROJ = A_OUT + BC
A_MLP = A_PROJ + 1
A_GATE = A_MLP + 2 * BC * FB
A_CHUNKS = A_GATE + BC
B_IQ, B_IKW, B_U, B_Q, B_K, B_V = 0, 2, 3, 5, 7, 9
B_OUT = 11
B_FF = B_OUT + BC
B_CHUNKS = B_FF + 2 * BC * FB

FIRST_GAINS = 248

AP_GMIX, AP_GMLP, AP_GPLE, AP_GSUB = 0, 8, 16, 24
AP_CONVW, AP_CONVB, AP_BA, AP_BX, AP_LRU = 25, 41, 45, 49, 53
AP_LAMQ, AP_LAMK, AP_INIT, AP_REST = 57, 185, 313, 314
AP_N = 315
BP_GPRE, BP_GPOST, BP_FPRE, BP_FPOST, BP_SCALE, BP_WPOOL = 0, 8, 16, 24, 32, 36
BP_N = BP_WPOOL + 4 * P
C_ID, C_ONES, C_TRI, C_CHUNK, C_FREQ, C_SIGN, C_CNT, C_GFIN, C_HPI, C_MHALF = 0, 128, 256, 384, 512, 513, 514, 578, 586, 587
C_N = C_MHALF + QT

TWO_PI = (1608.0 / 2**8, 254.0 / 2**17, -172.0 / 2**26)
TWO_PI += (2 * math.pi - sum(TWO_PI),)
ROUND = 1.5 * 2.0**23
PI_BELOW = 3.1415925


class Steps:

    def __init__(self, engine, semaphore):
        self.engine, self.semaphore, self.count = engine, semaphore, 0

    def mark(self, instruction):
        instruction.then_inc(self.semaphore, 1)
        self.count += 1

    def settle(self):
        self.engine.wait_ge(self.semaphore, self.count)


class Memory:
    pass


def build(nc, weights, params_a, params_b, gains, gates, embed, constants, positions, xt, out):
    with ExitStack() as ctx:
        def sb(name, shape, dtype=F32):
            return ctx.enter_context(nc.sbuf_tensor(name, shape, dtype))

        mem = Memory()
        mem.x = sb("x", [P, KT, S])
        mem.gh = sb("gh", [P, KT, S], F32R)
        mem.gl = sb("gl", [P, KT, S], F32R)
        mem.hh = sb("hh", [P, KT, S], F32R)
        mem.hl = sb("hl", [P, KT, S], F32R)
        mem.wr = sb("wr", [P, 2, CHUNK])
        mem.wh = sb("wh", [P, 2, CHUNK], F32R)
        mem.wl = sb("wl", [P, 2, CHUNK], F32R)
        mem.cst = sb("cst", [P, C_N])
        mem.par = sb("par", [P, max(AP_N, BP_N)])
        mem.rb = sb("rb", [P, S])
        mem.sq = sb("sq", [P, 2, S])
        mem.tmp = sb("tmp", [P, 4, S])
        mem.small = sb("small", [P, 256])
        mem.first_gains = mem.small[:, FIRST_GAINS:FIRST_GAINS + KT]
        mem.idb = sb("idb", [P, P], BF16)
        at = nc.sbuf_base
        mem.arena = sb("arena", [P, ARENA])
        mem.acc = mem.arena[:, ACC:ACC + S]
        mem.praw = nc.alloc_sbuf_tensor_at("praw", [P, 2, S], F32, offset=at + 4 * A1_XC)
        mem.ph = nc.alloc_sbuf_tensor_at("ph", [P, 2, S], F32R, offset=at + 4 * (A1_XC + 2 * S))
        mem.pl = nc.alloc_sbuf_tensor_at("pl", [P, 2, S], F32R, offset=at + 4 * (A1_XC + 4 * S))
        mem.ps = ctx.enter_context(nc.psum_tensor("ps", [P, 8, S], F32))

        prologue(nc, mem, constants, xt, weights, gains)
        with nc.Fori(0, DEPTH) as layer:
            first_stack_layer(nc, mem, layer, weights, params_a, gains, gates, embed, positions[0:P, :])
        final_norm(nc, mem)
        with nc.Fori(0, DEPTH) as layer:
            second_stack_layer(nc, mem, layer, weights, params_b, gains, positions[P:2 * P, :])
        epilogue(nc, mem, out)


def semaphores(nc, ctx, names):
    made = {name: ctx.enter_context(nc.semaphore(name)) for name in names.split()}
    numbers = [s.num for s in made.values()]
    assert numbers == list(range(numbers[0], numbers[-1] + 1))
    return made, range(numbers[0], numbers[-1] + 1)


def clear(nc, used):
    nc.gpsimd.sem_clear(used)
    nc.all_engine_barrier()


A1_QK, A1_XR, A1_CR, A1_XC = 0, 4096, 4096 + 2064, 4096 + 2064 + 1024
A1_R, A1_I, A1_GR = A1_XC + 2048, A1_XC + 4096, A1_XC + 6144
A1_GW = A1_QK + 6 * S
ACC = 14400
ARENA = 15392


def prologue(nc, mem, constants, xt, weights, gains):
    with ExitStack() as ctx:
        sem, used = semaphores(nc, ctx, "loaded chunk_loaded cast high low")
        with nc.Block() as block:
            @block.sync
            def _(sp):
                for c in range(2):
                    sp.dma_start(mem.wr[:, c, :], weights[c * P:(c + 1) * P, :]).then_inc(sem["chunk_loaded"], 16)
                sp.dma_start(mem.first_gains, gains[0:P, :]).then_inc(sem["loaded"], 16)
                sp.dma_start(mem.x[:, :, :], xt.rearrange("(k p) s -> p k s", p=P)).then_inc(sem["loaded"], 16)
                sp.dma_start(mem.cst[:, :], constants).then_inc(sem["loaded"], 16)
                sp.wait_ge(sem["loaded"], 48)

            @block.scalar
            def _(act):
                act.wait_ge(sem["chunk_loaded"], 32)
                for c in range(2):
                    act.activation(mem.wh[:, c, :], mem.wr[:, c, :], ACT.Copy).then_inc(sem["high"], 1)

            @block.vector
            def _(dve):
                for c in range(2):
                    dve.wait_ge(sem["high"], c + 1)
                    dve.tensor_tensor(mem.wl[:, c, :], mem.wr[:, c, :], mem.wh[:, c, :].bitcast(F32),
                                      ALU.subtract).then_inc(sem["low"], 1)
                dve.wait_ge(sem["loaded"], 48)
                dve.tensor_copy(mem.idb[:, :], mem.cst[:, C_ID:C_ID + P]).then_inc(sem["cast"], 1)
        clear(nc, used)


def epilogue(nc, mem, out):
    with ExitStack() as ctx:
        sem, used = semaphores(nc, ctx, "stored")
        with nc.Block() as block:
            @block.sync
            def _(sp):
                sp.dma_start(out.rearrange("(k p) s -> p k s", p=P), mem.x[:, :, :]).then_inc(sem["stored"], 16)
                sp.wait_ge(sem["stored"], 16)


def final_norm(nc, mem):
    x, sq, ps, cst, small, tmp = mem.x, mem.sq, mem.ps, mem.cst, mem.small, mem.tmp
    stat, ms, rs = ps[:, 4, 0:QT], small[:, 0:QT], small[:, QT:2 * QT]
    with ExitStack() as ctx:
        sem, used = semaphores(nc, ctx, "squared summed mean root diag spread scaled")
        with nc.Block() as block:
            @block.scalar
            def _(act):
                for k in range(KT):
                    if k >= 2:
                        act.wait_ge(sem["summed"], k - 1)
                    act.activation(sq[:, k % 2, :], x[:, k, :], ACT.Square).then_inc(sem["squared"], 1)

            @block.tensor
            def _(pe):
                for k in range(KT):
                    pe.wait_ge(sem["squared"], k + 1)
                    for i in range(QT):
                        last = pe.matmul(stat[:, i:i + 1], sq[:, k % 2, i * P:(i + 1) * P], cst[:, C_ONES:C_ONES + 1],
                                         start=(k == 0 and i == 0), stop=(k == KT - 1), skip_group_check=True)
                    last.then_inc(sem["summed"], 1)
                pe.wait_ge(sem["diag"], 1)
                pe.matmul(ps[:, 5, :], cst[:, C_ONES:C_ONES + P], tmp[:, 3, :], start=True, stop=True).then_inc(sem["spread"], 1)

            @block.gpsimd
            def _(pool):
                pool.wait_ge(sem["mean"], 1)
                pool.tensor_tensor(rs, ms, cst[:, C_MHALF:C_MHALF + QT], ALU.pow).then_inc(sem["root"], 1)

            @block.vector
            def _(dve):
                dve.wait_ge(sem["summed"], KT)
                dve.tensor_scalar(ms, stat, 1.0 / D, EPS, ALU.mult, ALU.add).then_inc(sem["mean"], 1)
                dve.wait_ge(sem["root"], 1)
                diagonals(dve, mem, rs).then_inc(sem["diag"], 1)
                dve.wait_ge(sem["spread"], 1)
                for k in range(KT):
                    dve.scalar_tensor_tensor(out=x[:, k, :], in0=x[:, k, :], scalar=cst[:, C_GFIN + k:C_GFIN + k + 1],
                                             in1=ps[:, 5, :], op0=ALU.mult, op1=ALU.mult).then_inc(sem["scaled"], 1)
        clear(nc, used)


def diagonals(dve, mem, rs):
    return dve.tensor_tensor(mem.tmp[:, 3, :].rearrange("p (i c) -> p i c", i=QT),
                             mem.cst[:, C_ID:C_ID + P].unsqueeze(1).broadcast_to([P, QT, P]),
                             rs.unsqueeze(2).broadcast_to([P, QT, P]), ALU.mult)



def once(_):
    return 0



def split_count(c):
    return c - 1


def load_chunk(sp, mem, sem, weights, row, c, per=once):
    row = sp.snap(row)
    if c >= 4:
        sp.wait_ge(sem["low"], split_count(c - 2) + per(2 * BC))
    loaded = (sem["loaded0"], sem["loaded1"])[c % 2]
    sp.dma_start(mem.wr[:, c % 2, :], weights[bass.ds(row, P), :]).then_inc(loaded, 16)


def load_next(sp, mem, sem, weights, gains, row, gain_row, c):
    load_chunk(sp, mem, sem, weights, row + P, c)
    load_chunk(sp, mem, sem, weights, row, c + 1)
    gain_row = sp.snap(gain_row)
    sp.wait_ge(sem["gain_low"], KT)
    sp.dma_start(mem.first_gains, gains[bass.ds(gain_row, P), :]).then_inc(sem["next_gains"], 16)
    sp.wait_ge(sem["next_gains"], 16)


def split_high(act, mem, sem, c, used, per=once):
    act.wait_ge((sem["loaded0"], sem["loaded1"])[c % 2], 16 * (c // 2) + per(16 * BC))
    act.wait_ge(sem["product"], used + per(4 * BC))
    act.activation(mem.wh[:, c % 2, :], mem.wr[:, c % 2, :], ACT.Copy).then_inc(sem["high"], 1)


def split_low(dve, mem, sem, c, per=once):
    dve.wait_ge(sem["high"], split_count(c) + per(2 * BC))
    dve.tensor_tensor(mem.wl[:, c % 2, :], mem.wr[:, c % 2, :], mem.wh[:, c % 2, :].bitcast(F32),
                      ALU.subtract).then_inc(sem["low"], 1)


def three_passes(pe, out, w_high, w_low, high, low, first, last, swap=False):
    pairs = ((w_high, high), (w_high, low), (w_low, high))
    if swap:
        pairs = ((high, w_high), (low, w_high), (high, w_low))
    for n, (stationary, moving) in enumerate(pairs):
        done = pe.matmul(out, stationary, moving, start=(first and n == 0), stop=(last and n == 2),
                         skip_group_check=True)
    return done


def product_tile(pe, mem, sem, c, column, tile, high, low, order=range(KT), before=None, width=P, per=once):
    if column == 0 and c >= 2:
        pe.wait_ge(sem["low"], split_count(c) + per(2 * BC))
    if tile >= 4:
        pe.wait_ge(sem["drained"], tile - 3 + per(4 * BC))
    wh = mem.wh[:, c % 2, :].rearrange("p (k n) -> p k n", k=KT)
    wl = mem.wl[:, c % 2, :].rearrange("p (k n) -> p k n", k=KT)
    order = list(order)
    for k in order:
        if before:
            before(k)
        last = three_passes(pe, mem.ps[0:width, tile % 4, :], wh[:, k, column:column + width], wl[:, k, column:column + width],
                            high[:, k, :], low[:, k, :], k == order[0], k == order[-1])
    last.then_inc(sem["product"], 1)


def first_two_chunks(pe, mem, sem, c0, tile, n, before):
    wh, wl = ([w[:, c, :].rearrange("p (k n) -> p k n", k=KT) for c in range(2)] for w in (mem.wh, mem.wl))

    def part(k, c):
        if k == 0 and c0:
            pe.wait_ge(sem["low"], split_count(c0 + c))
        s = (c0 + c) % 2
        for t in range(2):
            at = slice(P * t, P * (t + 1))
            last = three_passes(pe, mem.ps[:, (tile + 2 * c + t) % 4, :], wh[s][:, k, at], wl[s][:, k, at],
                                mem.gh[:, k, :], mem.gl[:, k, :], k == 0, k == KT - 1)
            if k == KT - 1:
                last.then_inc(sem["product"], 1)

    for k in range(KT // 2):
        before(k)
        part(k, 0)
        part(k, 1)
    for k in range(KT // 2, KT):
        before(k)
        part(k, 0)
    sum_squares(pe, mem, sem, n)
    for k in range(KT // 2, KT):
        part(k, 1)
        if k == KT - 3:
            spread_root(pe, mem, sem, n)


def token_tile(pe, mem, sem, c, i, tile):
    if i == 0:
        pe.wait_ge(sem["low"], split_count(c))
    pe.wait_ge(sem["drained"], tile - 3)
    wh = mem.wh[:, c % 2, :].rearrange("p (k n) -> p k n", k=KT)
    wl = mem.wl[:, c % 2, :].rearrange("p (k n) -> p k n", k=KT)
    for k in range(KT):
        last = three_passes(pe, mem.ps[:, tile % 4, 0:CW], wh[:, k, :], wl[:, k, :],
                            mem.gh[:, k, i * P:(i + 1) * P], mem.gl[:, k, i * P:(i + 1) * P], k == 0, k == KT - 1, swap=True)
    last.then_inc(sem["product"], 1)



GATHERS = KT - 2


def square_slice(act, mem, sem, n, k, source):
    if k >= 2:
        act.wait_ge(sem["gathered"], GATHERS * n + max(1, k - 2))
    elif n and k == 0:
        act.wait_ge(sem["gathered"], GATHERS * n)
    elif n:
        act.wait_ge(sem["summed"], n)
    act.activation(mem.sq[:, k % 2, :], source[:, k, :], ACT.Square).then_inc(sem["squared"], 1)


def gather_squares(pool, mem, sem, n):
    for k in range(1, KT - 1):
        pool.wait_ge(sem["squared"], KT * n + k + 1)
        if k == 1 and n:
            pool.wait_ge(sem["summed"], n)
        if k > 1:
            pool.wait_ge(sem["gathered"], GATHERS * n + k - 1)
        pool.tensor_tensor(mem.acc, mem.sq[:, 0, :] if k == 1 else mem.acc, mem.sq[:, k % 2, :], ALU.add)\
            .then_inc(sem["gathered"], 1)


def sum_squares(pe, mem, sem, n):
    if n:
        pe.wait_ge(sem["mean"], n)
    for squares, ready, count, start in ((mem.acc, "gathered", GATHERS * (n + 1), True),
                                         (mem.sq[:, 1, :], "squared", KT * (n + 1), False)):
        pe.wait_ge(sem[ready], count)
        for i in range(QT):
            last = pe.matmul(mem.ps[:, 4, i:i + 1], squares[:, i * P:(i + 1) * P], mem.cst[:, C_ONES:C_ONES + 1],
                             start=(start and i == 0), stop=not start, skip_group_check=True)
    last.then_inc(sem["summed"], 1)


def mean_square(dve, mem, sem, n):
    dve.wait_ge(sem["summed"], n + 1)
    dve.tensor_scalar(mem.small[:, 0:QT], mem.ps[:, 4, 0:QT], 1.0 / D, EPS, ALU.mult, ALU.add).then_inc(sem["mean"], 1)


def one_over_root(pool, mem, sem, n):
    pool.wait_ge(sem["mean"], n + 1)
    pool.tensor_tensor(mem.small[:, QT:2 * QT], mem.small[:, 0:QT], mem.cst[:, C_MHALF:C_MHALF + QT],
                       ALU.pow).then_inc(sem["root"], 1)


def root_diagonals(dve, mem, sem, n):
    dve.wait_ge(sem["root"], n + 1)
    diagonals(dve, mem, mem.small[:, QT:2 * QT]).then_inc(sem["diag"], 1)


def spread_root(pe, mem, sem, n):
    pe.wait_ge(sem["diag"], n + 1)
    pe.matmul(mem.ps[:, 5, :], mem.cst[:, C_ONES:C_ONES + P], mem.tmp[:, 3, :], start=True, stop=True).then_inc(sem["spread"], 1)


def keep_root(act, mem, sem, n):
    act.wait_ge(sem["spread"], n + 1)
    act.activation(mem.rb[:, :], mem.ps[:, 5, :], ACT.Copy).then_inc(sem["kept"], 1)


def gain_high(act, mem, sem, k, gains):
    act.activation(mem.gh[:, k, :], mem.x[:, k, :], ACT.Copy, scale=gains[:, k:k + 1]).then_inc(sem["gain_high"], 1)


def gain_low(dve, mem, sem, n, k, gains):
    dve.wait_ge(sem["gain_high"], KT * n + k + 1)
    dve.scalar_tensor_tensor(out=mem.gl[:, k, :], in0=mem.x[:, k, :], scalar=gains[:, k:k + 1],
                             in1=mem.gh[:, k, :].bitcast(F32), op0=ALU.mult, op1=ALU.subtract).then_inc(sem["gain_low"], 1)



def rotary_angles(dve, steps, mem, whole, left):
    freq = mem.cst[:, C_FREQ:C_FREQ + 1]
    steps.mark(dve.tensor_copy(left, whole.bitcast(I32)))
    steps.settle()
    steps.mark(dve.tensor_scalar(left, left, freq, None, ALU.mult))
    steps.settle()
    steps.mark(dve.tensor_scalar(whole, left, 1.0 / (2 * math.pi), ROUND, ALU.mult, ALU.add))
    steps.settle()
    steps.mark(dve.tensor_scalar(whole, whole, ROUND, None, ALU.subtract))
    for part in TWO_PI:
        steps.settle()
        steps.mark(dve.scalar_tensor_tensor(out=left, in0=whole, scalar=-part, in1=left, op0=ALU.mult, op1=ALU.add))
    steps.settle()
    steps.mark(dve.tensor_scalar(left, left, PI_BELOW, -PI_BELOW, ALU.min, ALU.max))
    steps.settle()
    return dve.scalar_tensor_tensor(out=whole, in0=left, scalar=-1.0, in1=left, op0=ALU.mult, op1=ALU.max)


SWAP = [(i + ROT_HALF) % (2 * ROT_HALF) if i < 2 * ROT_HALF else i for i in range(32)]


def rotate(dve, steps, mem, sem, tile, out, cos, sin, width=P):
    dve.wait_ge(sem["product"], tile + 1)
    acc = mem.ps[0:width, tile % 4, :]
    steps.settle()
    steps.mark(dve.stream_shuffle(mem.tmp[0:width, 2, :], acc, SWAP))
    dve.tensor_tensor(out, acc, cos[0:width], ALU.mult).then_inc(sem["drained"], 1)
    steps.settle()
    steps.mark(dve.tensor_tensor(mem.tmp[0:width, 2, :], mem.tmp[0:width, 2, :], sin[0:width], ALU.mult))
    steps.settle()
    dve.wait_ge(sem["drained"], tile + 1)
    steps.mark(dve.tensor_tensor(out, out, mem.tmp[0:width, 2, :], ALU.add))



A_TILE = {c: 2 * c for c in range(A_V)}
A_TILE.update({A_V: 16, A_V + 1: 20, A_V + 2: 24})
A_TILE.update({c: 24 + 2 * (c - A_OUT) for c in range(A_OUT, A_PROJ + 1)})
A_TILE.update({c: 40 + 2 * (c - A_MLP) for c in range(A_MLP, A_CHUNKS + 1)})

SM_OMS, SM_ORS, SM_C8, SM_NC8, SM_X, SM_E, SM_S, SM_S2, SM_PL, SM_LAM, SM_GS = 8, 12, 16, 20, 24, 28, 32, 36, 40, 44, 50
SM_MAX, SM_NEG, SM_SUM, SM_INV = 56, 60, 64, 68
LOG1P = (1 / 17, 1 / 15, 1 / 13, 1 / 11, 1 / 9, 1 / 7, 1 / 5, 1 / 3, 1.0)


def a_used(c):
    return A_TILE[c - 1]


def first_stack_layer(nc, mem, layer, weights, params, gains, gates, embed, positions):
    ar, ps, cst, par, small, tmp, x = mem.arena, mem.ps, mem.cst, mem.par, mem.small, mem.tmp, mem.x
    qk = ar[:, A1_QK:A1_QK + 4096].rearrange("p (t s) -> p t s", s=S)
    xr = ar[:, A1_XR:A1_XR + 4 * (S + 4)].rearrange("p (t s) -> p t s", s=S + 4)
    v = ar[:, A1_XR:A1_XR + 4 * S].rearrange("p (t s) -> p t s", s=S)
    cos, sin = ar[:, A1_CR:A1_CR + S], ar[:, A1_CR + S:A1_CR + 2 * S]
    xc, rr, ii, gr = (ar[:, a:a + 2048].rearrange("p (t s) -> p t s", s=S) for a in (A1_XC, A1_R, A1_I, A1_GR))
    gw = ar[:, A1_GW:A1_GW + 2 * S].rearrange("p (g t n) -> p g t n", g=2, t=4)
    prob = ar[:, A1_XC:A1_XC + 2048].rearrange("p (b c s) -> p b c s", b=2, c=2)
    mixed = ar[:, A1_R:A1_R + 1024].rearrange("p (b s) -> p b s", b=2)
    head_out = ar[:, A1_R + 1024:A1_R + 2048].rearrange("p (b s) -> p b s", b=2)
    pt = ar[:, A1_I:A1_I + 4096].rearrange("p (b k s) -> p b k s", b=2, k=QT)
    proj = qk
    ident, ones = cst[:, C_ID:C_ID + P], cst[:, C_ONES:C_ONES + P]
    STEPS = 4 * HEADS1

    with ExitStack() as ctx:
        sem, used = semaphores(nc, ctx, (
            "loaded0 loaded1 next_gains vectors positioned embedded high low product drained squared gathered summed mean root diag spread kept "
            "gain_high gain_low own act_own tables softexp lamexp rates conv gate_product gated gelued gated_input decayed gain_ready "
            "rooted y_ready y_high y_low scored maxed exped mixed_done turned untangled weighted copied o_squared o_summed o_mean o_root "
            "o_diag o_spread o_ready o_high o_low embed_high embed_low hidden hidden_high hidden_low gate_in gate_out padded"))
        with nc.Block() as block:

            @block.sync
            def _(sp):
                def chunk(c, per=once, j=None):
                    row = (layer * A_CHUNKS + c) * P if j is None else (layer * A_CHUNKS + c + j * (2 * BC)) * P
                    load_chunk(sp, mem, sem, weights, row, c, per)

                rows = sp.snap(layer * P)
                sp.dma_start(par[:, 0:AP_N], params[bass.ds(rows, P), :]).then_inc(sem["vectors"], 16)
                sp.dma_start(tmp[:, 0, :].bitcast(I32), positions).then_inc(sem["positioned"], 16)
                sp.dma_start(ar[:, A1_GW:A1_GW + 2 * S], gates[bass.ds(rows, P), :]).then_inc(sem["positioned"], 16)
                for c in range(2, A_OUT + 2):
                    chunk(c)
                sp.wait_ge(sem["copied"], HEADS1)
                sp.dma_start(mem.praw[:, :, :].rearrange("p k s -> p (k s)"), embed[bass.ds(rows, P), :]).then_inc(sem["embedded"], 16)
                for c in range(A_OUT + 2, A_MLP):
                    chunk(c)
                with sp.Fori(0, FB) as j:
                    for i in range(2 * BC):
                        chunk(A_MLP + i, lambda n: j * n, j)
                for c in range(A_GATE, A_CHUNKS):
                    chunk(c)
                load_next(sp, mem, sem, weights, gains, (layer + 1) * (A_CHUNKS * P), (layer + 1) * P, A_CHUNKS)

            @block.gpsimd
            def _(pool):
                pool.memset(xr[:, :, 0:4], 0.0).then_inc(sem["padded"], 1)
                gather_squares(pool, mem, sem, 0)
                one_over_root(pool, mem, sem, 0)
                for t in range(4):
                    pool.wait_ge(sem["gated"], 2 * (t + 1))
                    pool.tensor_tensor(xc[:, t, :], xc[:, t, :], ii[:, t, :], ALU.mult).then_inc(sem["gated_input"], 1)
                for h in range(HEADS1):
                    if h in (0, 1):
                        if h == 0:
                            pool.wait_ge(sem["low"], split_count(A_OUT - 1))
                        split_low(pool, mem, sem, A_OUT + h)
                    pool.wait_ge(sem["o_mean"], h + 1)
                    pool.tensor_tensor(small[:, SM_ORS:SM_ORS + QT], small[:, SM_OMS:SM_OMS + QT],
                                       cst[:, C_MHALF:C_MHALF + QT], ALU.pow).then_inc(sem["o_root"], 1)
                for n in (1, 2):
                    gather_squares(pool, mem, sem, n)
                    one_over_root(pool, mem, sem, n)

            @block.scalar
            def _(act):
                for k in range(KT):
                    gain_high(act, mem, sem, k, mem.first_gains)
                    square_slice(act, mem, sem, 0, k, x)
                split_high(act, mem, sem, 2, a_used(2))
                keep_root(act, mem, sem, 0)
                act.wait_ge(sem["tables"], 1)
                act.activation(sin, tmp[:, 1, :], ACT.Sin, scale=cst[:, C_SIGN:C_SIGN + 1]).then_inc(sem["tables"], 1)
                act.activation(cos, tmp[:, 0, :], ACT.Sin, scale=-1.0, bias=cst[:, C_HPI:C_HPI + 1]).then_inc(sem["tables"], 1)
                split_high(act, mem, sem, 3, a_used(3))
                act.wait_ge(sem["vectors"], 16)
                for t in range(4):
                    if t == 2:
                        split_high(act, mem, sem, 4, a_used(4))
                    for g, (gate, bias) in enumerate(((rr, AP_BA), (ii, AP_BX))):
                        act.wait_ge(sem["gate_product"], 2 * t + g + 1)
                        act.activation(gate[:, t, :], ps[:, 6 + g, :], ACT.Sigmoid,
                                       bias=par[:, bias + t:bias + t + 1]).then_inc(sem["gated"], 1)
                act.wait_ge(sem["softexp"], 1)
                act.activation(small[:, SM_E:SM_E + 4], small[:, SM_X:SM_X + 4], ACT.Exp, scale=-1.0).then_inc(sem["act_own"], 1)
                act.activation(small[:, SM_LAM + 2:SM_LAM + 4], small[:, SM_LAM:SM_LAM + 2], ACT.Exp).then_inc(sem["lamexp"], 1)
                for t in range(4):
                    act.wait_ge(sem["drained"], A_TILE[A_GR] + t + 1)
                    act.activation(gr[:, t, :], gr[:, t, :], ACT.Gelu_apprx_tanh).then_inc(sem["gelued"], 1)
                split_high(act, mem, sem, 5, a_used(5))
                act.wait_ge(sem["rates"], 2)
                for t in range(4):
                    act.wait_ge(sem["gated_input"], t + 1)
                    act.wait_ge(sem["gated"], 8)
                    act.activation(ii[:, t, :], rr[:, t, :], ACT.Tanh, scale=small[:, SM_C8 + t:SM_C8 + t + 1]).then_inc(sem["decayed"], 1)
                    act.activation(rr[:, t, :], rr[:, t, :], ACT.Exp, scale=small[:, SM_NC8 + t:SM_NC8 + t + 1]).then_inc(sem["decayed"], 1)
                split_high(act, mem, sem, 6, a_used(6))
                for t in range(4):
                    if t >= 2:
                        act.wait_ge(sem["gain_ready"], t - 1)
                    act.wait_ge(sem["decayed"], 2 * t + 2)
                    act.wait_ge(sem["summed"], 1)
                    act.activation(mem.sq[:, t % 2, :], rr[:, t, :], ACT.Square).then_inc(sem["decayed"], 1)
                split_high(act, mem, sem, 7, a_used(7))
                for t in range(4):
                    act.wait_ge(sem["gain_ready"], t + 1)
                    act.activation(ii[:, t, :], ii[:, t, :], ACT.Sqrt).then_inc(sem["rooted"], 1)
                split_high(act, mem, sem, 8, a_used(8))
                split_high(act, mem, sem, 9, a_used(9))
                for t in range(4):
                    act.wait_ge(sem["y_ready"], t + 1)
                    act.activation(mem.hh[:, 4 + t, :], tmp[:, 1, :], ACT.Copy).then_inc(sem["y_high"], 1)

                def exponents(s):
                    h, i = divmod(s, QT)
                    n = P * (i + 1)
                    act.wait_ge(sem["maxed"], s + 1)
                    if s == 0:
                        act.wait_ge(sem["y_low"], 4)
                    if s >= 2:
                        act.wait_ge(sem["mixed_done"], s - 1)
                    for c in range(2):
                        act.activation(prob[:, s % 2, c, 0:n], ps[:, 2 * (s % 2) + c, 0:n], ACT.Exp, scale=DH ** -0.5,
                                       bias=small[:, SM_NEG + 2 * (s % 2) + c:SM_NEG + 2 * (s % 2) + c + 1],
                                       accum_out=small[:, SM_SUM + 2 * (s % 2) + c:SM_SUM + 2 * (s % 2) + c + 1]).then_inc(sem["exped"], 1)

                def untangle(s):
                    h, i = divmod(s, QT)
                    act.wait_ge(sem["turned"], s + 1)
                    if h >= 2:
                        act.wait_ge(sem["weighted"], h - 1)
                    act.activation(pt[:, h % 2, 0:i + 1, P * i:P * (i + 1)],
                                   ps[:, 5, 0:P * (i + 1)].rearrange("p (k q) -> p k q", q=P), ACT.Copy).then_inc(sem["untangled"], 1)

                def head_squares(h):
                    act.wait_ge(sem["weighted"], h + 1)
                    if h >= 2:
                        act.wait_ge(sem["o_ready"], h - 1)
                        act.wait_ge(sem["o_summed"], h - 1)
                    act.activation(head_out[:, h % 2, :], ps[:, 6, :], ACT.Copy).then_inc(sem["copied"], 1)
                    act.activation(mem.sq[:, h % 2, :], ps[:, 6, :], ACT.Square).then_inc(sem["o_squared"], 1)

                def head_high(h):
                    act.wait_ge(sem["o_ready"], h + 1)
                    act.activation(mem.hh[:, h, :], tmp[:, 1, :], ACT.Copy).then_inc(sem["o_high"], 1)

                exponents(0)
                for s in range(STEPS):
                    if s + 1 < STEPS:
                        exponents(s + 1)
                    h, i = divmod(s, QT)
                    if h and i == 1:
                        head_squares(h - 1)
                    untangle(s)
                    if h > 1 and i == 0:
                        head_high(h - 2)
                    if s in (4, 8):
                        c = A_OUT + s // 4 - 1
                        split_high(act, mem, sem, c, a_used(c))
                head_high(HEADS1 - 2)
                head_squares(HEADS1 - 1)
                head_high(HEADS1 - 1)

                def own_slice(n, k, tile, gains):
                    act.wait_ge(sem["drained"], tile + 1)
                    gain_high(act, mem, sem, k, gains)
                    square_slice(act, mem, sem, n, k, x)

                for c in range(A_OUT, A_PROJ):
                    if c + 1 >= A_OUT + 2:
                        split_high(act, mem, sem, c + 1, a_used(c + 1))
                    for t in range(2):
                        k = 2 * (c - A_OUT) + t
                        own_slice(1, k, A_TILE[c] + t, par[:, AP_GMLP:AP_GMLP + KT])
                    if c == A_OUT:
                        act.wait_ge(sem["embedded"], 16)
                        act.wait_ge(sem["o_low"], HEADS1)
                        act.activation(mem.ph[:, :, :], mem.praw[:, :, :], ACT.Copy).then_inc(sem["embed_high"], 1)
                split_high(act, mem, sem, A_MLP, a_used(A_MLP))
                keep_root(act, mem, sem, 1)

                def mlp_first(c0, per, j):
                    for i in range(BC):
                        split_high(act, mem, sem, c0 + i + 1, a_used(c0 + i + 1), per)
                        for t in range(2):
                            act.wait_ge(sem["hidden"], 2 * i + t + 1 + j * KT)
                            act.activation(mem.hh[:, 2 * i + t, :], tmp[:, 1, :], ACT.Copy).then_inc(sem["hidden_high"], 1)

                with act.Fori(0, FB - 1) as j:
                    def per(n):
                        return j * n

                    mlp_first(A_MLP, per, j)
                    for i in range(BC, 2 * BC):
                        split_high(act, mem, sem, A_MLP + i + 1, a_used(A_MLP + i + 1), per)
                c0 = A_GATE - 2 * BC
                mlp_first(c0, once, FB - 1)
                for c in range(c0 + BC, A_GATE):
                    split_high(act, mem, sem, c + 1, a_used(c + 1))
                    for t in range(2):
                        own_slice(2, 2 * (c - c0 - BC) + t, A_TILE[c] + t, par[:, AP_GPLE:AP_GPLE + KT])
                split_high(act, mem, sem, A_GATE + 1, a_used(A_GATE + 1))
                keep_root(act, mem, sem, 2)
                for c in range(A_GATE, A_CHUNKS):
                    if c > A_GATE:
                        split_high(act, mem, sem, c + 1, a_used(c + 1))
                    for t in range(2):
                        act.wait_ge(sem["drained"], A_TILE[c] + t + 1)
                        act.activation(tmp[:, 1, :], tmp[:, 0, :], ACT.Sigmoid).then_inc(sem["gate_out"], 1)
                split_high(act, mem, sem, A_CHUNKS + 1, a_used(A_CHUNKS + 1))

            @block.vector
            def _(dve):
                own = Steps(dve, sem['own'])
                mlp_gains, gate_gains = par[:, AP_GMLP:AP_GMLP + KT], par[:, AP_GPLE:AP_GPLE + KT]
                for k in range(KT):
                    gain_low(dve, mem, sem, 0, k, mem.first_gains)
                dve.wait_ge(sem["positioned"], 32)
                rotary_angles(dve, own, mem, tmp[:, 0, :], tmp[:, 1, :]).then_inc(sem["tables"], 1)
                mean_square(dve, mem, sem, 0)
                root_diagonals(dve, mem, sem, 0)

                def drain(out, tile):
                    dve.wait_ge(sem["product"], tile + 1)
                    dve.tensor_tensor(out, ps[:, tile % 4, :], mem.rb[:, :], ALU.mult).then_inc(sem["drained"], 1)

                def convolve(t):
                    for tap in range(CONV - 1, -1, -1):
                        taps = par[:, AP_CONVW + 4 * tap + t:AP_CONVW + 4 * tap + t + 1]
                        window = xr[:, t, 1 + tap:1 + tap + S]
                        if tap == CONV - 1:
                            own.mark(dve.tensor_scalar(xc[:, t, :], window, taps, par[:, AP_CONVB + t:AP_CONVB + t + 1], ALU.mult, ALU.add))
                            own.settle()
                            continue
                        last = dve.scalar_tensor_tensor(out=xc[:, t, :], in0=window, scalar=taps, in1=xc[:, t, :],
                                                        op0=ALU.mult, op1=ALU.add)
                        if tap:
                            own.mark(last)
                            own.settle()
                    last.then_inc(sem["conv"], 1)

                split_low(dve, mem, sem, 2)
                dve.wait_ge(sem["kept"], 1)
                dve.wait_ge(sem["vectors"], 16)
                dve.wait_ge(sem["padded"], 1)
                for c in (A_XR, A_XR + 1):
                    for t in range(2):
                        drain(xr[:, 2 * c + t, 4:4 + S], A_TILE[c] + t)
                for t in range(4):
                    dve.wait_ge(sem["drained"], t + 1)
                    convolve(t)
                    if t == 1:
                        split_low(dve, mem, sem, 3)

                sx, se, ss, s2, spl = (small[:, a:a + 4] for a in (SM_X, SM_E, SM_S, SM_S2, SM_PL))
                lru = par[:, AP_LRU:AP_LRU + 4]
                own.mark(dve.scalar_tensor_tensor(out=sx, in0=lru, scalar=-1.0, in1=lru, op0=ALU.mult, op1=ALU.max))
                dots = tmp[:, 3, 0:2 * DH]
                dve.wait_ge(sem["spread"], 1)
                own.mark(dve.tensor_tensor(dots, par[:, AP_LAMQ:AP_LAMQ + 2 * DH], par[:, AP_LAMK:AP_LAMK + 2 * DH], ALU.mult))
                own.settle()
                dve.tensor_reduce(small[:, SM_LAM:SM_LAM + 2], dots.rearrange("p (a d) -> p a d", a=2), AX.X, ALU.add)\
                    .then_inc(sem["softexp"], 1)

                for c in (A_GR, A_GR + 1):
                    if c > A_GR:
                        split_low(dve, mem, sem, c + 1)
                    for t in range(2):
                        drain(gr[:, 2 * (c - A_GR) + t, :], A_TILE[c] + t)
                dve.wait_ge(sem["act_own"], 1)
                dve.wait_ge(sem["lamexp"], 1)
                own.mark(dve.tensor_scalar(ss, se, 2.0, None, ALU.add))
                own.settle()
                own.mark(dve.reciprocal(ss, ss))
                own.settle()
                own.mark(dve.tensor_tensor(ss, ss, se, ALU.mult))
                own.settle()
                own.mark(dve.tensor_tensor(s2, ss, ss, ALU.mult))
                own.settle()
                own.mark(dve.tensor_scalar(spl, s2, LOG1P[0], None, ALU.mult))
                for term in LOG1P[1:-1]:
                    own.settle()
                    own.mark(dve.scalar_tensor_tensor(out=spl, in0=spl, scalar=term, in1=s2, op0=ALU.add, op1=ALU.mult))
                own.settle()
                own.mark(dve.scalar_tensor_tensor(out=spl, in0=spl, scalar=1.0, in1=ss, op0=ALU.add, op1=ALU.mult))
                own.mark(dve.tensor_scalar(sx, lru, -1.0, 0.0, ALU.mult, ALU.max))
                own.settle()
                own.mark(dve.scalar_tensor_tensor(out=spl, in0=spl, scalar=2.0, in1=sx, op0=ALU.mult, op1=ALU.add))
                own.settle()
                dve.tensor_scalar(small[:, SM_C8:SM_C8 + 4], spl, 8.0, None, ALU.mult).then_inc(sem["rates"], 1)
                dve.tensor_scalar(small[:, SM_NC8:SM_NC8 + 4], spl, -8.0, None, ALU.mult).then_inc(sem["rates"], 1)
                nlam = small[:, SM_LAM + 4:SM_LAM + 5]
                own.mark(dve.tensor_tensor(nlam, small[:, SM_LAM + 3:SM_LAM + 4], small[:, SM_LAM + 2:SM_LAM + 3], ALU.subtract))
                own.settle()
                own.mark(dve.tensor_scalar(nlam, nlam, par[:, AP_INIT:AP_INIT + 1], None, ALU.subtract))
                gsub = small[:, SM_GS:SM_GS + 1]
                own.mark(dve.tensor_scalar(gsub, par[:, AP_GSUB:AP_GSUB + 1], par[:, AP_REST:AP_REST + 1], None, ALU.mult))


                dve.wait_ge(sem["tables"], 3)
                own.mark(dve.tensor_tensor(sin, sin, mem.rb[:, :], ALU.mult))
                own.mark(dve.tensor_tensor(cos, cos, mem.rb[:, :], ALU.mult))
                own.settle()

                def gain(t):
                    dve.wait_ge(sem["decayed"], 8 + t + 1)
                    dve.scalar_tensor_tensor(out=ii[:, t, :], in0=mem.sq[:, t % 2, :], scalar=1.0, in1=ii[:, t, :],
                                             op0=ALU.add, op1=ALU.mult).then_inc(sem["gain_ready"], 1)

                def recur(t):
                    dve.wait_ge(sem["rooted"], t + 1)
                    dve.wait_ge(sem["gated_input"], t + 1)
                    own.mark(dve.tensor_tensor(xc[:, t, :], xc[:, t, :], ii[:, t, :], ALU.mult))
                    own.settle()
                    own.mark(dve.tensor_tensor_scan(ii[:, t, :], rr[:, t, :], xc[:, t, :], 0.0, ALU.mult, ALU.add))
                    own.settle()
                    dve.wait_ge(sem["gelued"], t + 1)
                    dve.tensor_tensor(tmp[:, 1, :], ii[:, t, :], gr[:, t, :], ALU.mult).then_inc(sem["y_ready"], 1)
                    dve.wait_ge(sem["y_high"], t + 1)
                    dve.tensor_tensor(mem.hl[:, 4 + t, :], tmp[:, 1, :], mem.hh[:, 4 + t, :].bitcast(F32),
                                      ALU.subtract).then_inc(sem["y_low"], 1)

                for c in range(A_Q, A_V):
                    split_low(dve, mem, sem, c + 1)
                    for t in range(2):
                        rotate(dve, own, mem, sem, A_TILE[c] + t, qk[:, 2 * (c - A_Q) + t, :], cos, sin)
                    if c == A_Q + 1:
                        for t in range(4):
                            gain(t)
                recur(0)
                for c in (A_V, A_V + 1):
                    if c == A_V:
                        split_low(dve, mem, sem, c + 1)
                        own.settle()
                    else:
                        recur(3)
                    for i in range(QT):
                        tile = A_TILE[c] + i
                        dve.wait_ge(sem["product"], tile + 1)
                        dve.tensor_scalar(v[:, i, (c - A_V) * CW:(c - A_V + 1) * CW], ps[:, tile % 4, 0:CW],
                                          small[:, QT + i:QT + i + 1], None, ALU.mult).then_inc(sem["drained"], 1)
                    if c == A_V:
                        recur(1)
                        recur(2)

                def maxima(s):
                    n, b = P * (s % QT + 1), s % 2
                    dve.wait_ge(sem["scored"], s + 1)
                    own.mark(dve.tensor_reduce(small[:, SM_MAX + 2 * b:SM_MAX + 2 * b + 2], ps[:, 2 * b:2 * b + 2, 0:n], AX.X, ALU.max))
                    own.settle()
                    dve.tensor_scalar(small[:, SM_NEG + 2 * b:SM_NEG + 2 * b + 2], small[:, SM_MAX + 2 * b:SM_MAX + 2 * b + 2],
                                      -(DH ** -0.5), None, ALU.mult).then_inc(sem["maxed"], 1)

                def mix(s):
                    n, b = P * (s % QT + 1), s % 2
                    inv = small[:, SM_INV + 2 * b:SM_INV + 2 * b + 2]
                    dve.wait_ge(sem["exped"], 2 * (s + 1))
                    own.mark(dve.reciprocal(inv, small[:, SM_SUM + 2 * b:SM_SUM + 2 * b + 2]))
                    own.settle()
                    own.mark(dve.tensor_tensor(inv[:, 1:2], inv[:, 1:2], nlam, ALU.mult))
                    if s >= 2:
                        dve.wait_ge(sem["turned"], s - 1)
                    own.mark(dve.tensor_scalar(mixed[:, b, 0:n], prob[:, b, 0, 0:n], inv[:, 0:1], None, ALU.mult))
                    own.settle()
                    dve.scalar_tensor_tensor(out=mixed[:, b, 0:n], in0=prob[:, b, 1, 0:n], scalar=inv[:, 1:2],
                                             in1=mixed[:, b, 0:n], op0=ALU.mult, op1=ALU.add).then_inc(sem["mixed_done"], 1)

                def head_mean(h):
                    dve.wait_ge(sem["o_summed"], h + 1)
                    dve.tensor_scalar(small[:, SM_OMS:SM_OMS + QT], ps[:, 4, 8:8 + QT], 1.0 / P, EPS, ALU.mult, ALU.add)\
                        .then_inc(sem["o_mean"], 1)
                    dve.wait_ge(sem["o_root"], h + 1)
                    if h:
                        dve.wait_ge(sem["o_spread"], h)
                    diagonals(dve, mem, small[:, SM_ORS:SM_ORS + QT]).then_inc(sem["o_diag"], 1)

                def head_norm(h):
                    if h:
                        dve.wait_ge(sem["o_low"], h)
                    dve.wait_ge(sem["o_spread"], h + 1)
                    dve.wait_ge(sem["copied"], h + 1)
                    dve.scalar_tensor_tensor(out=tmp[:, 1, :], in0=head_out[:, h % 2, :], scalar=gsub, in1=ps[:, 7, :],
                                             op0=ALU.mult, op1=ALU.mult).then_inc(sem["o_ready"], 1)

                def head_low(h):
                    dve.wait_ge(sem["o_high"], h + 1)
                    dve.tensor_tensor(mem.hl[:, h, :], tmp[:, 1, :], mem.hh[:, h, :].bitcast(F32),
                                      ALU.subtract).then_inc(sem["o_low"], 1)

                maxima(0)
                maxima(1)
                for s in range(STEPS):
                    mix(s)
                    if s + 2 < STEPS:
                        maxima(s + 2)
                    h, i = divmod(s, QT)
                    if h > 1 and i == 0:
                        head_norm(h - 2)
                    if h > 1 and i == 1:
                        head_low(h - 2)
                    if h and i == 2:
                        head_mean(h - 1)
                head_norm(HEADS1 - 2)
                head_low(HEADS1 - 2)
                head_mean(HEADS1 - 1)
                head_norm(HEADS1 - 1)
                head_low(HEADS1 - 1)

                def add_to_x(tile, k, per=once):
                    dve.wait_ge(sem["product"], tile + 1 + per(4 * BC))
                    dve.tensor_tensor(x[:, k, :], x[:, k, :], ps[:, tile % 4, :], ALU.add).then_inc(sem["drained"], 1)

                dve.wait_ge(sem["low"], split_count(A_OUT + 1))
                for c in range(A_OUT, A_PROJ):
                    if c + 1 >= A_OUT + 2:
                        split_low(dve, mem, sem, c + 1)
                    for t in range(2):
                        k = 2 * (c - A_OUT) + t
                        add_to_x(A_TILE[c] + t, k)
                        gain_low(dve, mem, sem, 1, k, mlp_gains)
                    if c == A_OUT:
                        dve.wait_ge(sem["embed_high"], 1)
                        dve.tensor_tensor(mem.pl[:, :, :], mem.praw[:, :, :], mem.ph[:, :, :].bitcast(F32),
                                          ALU.subtract).then_inc(sem["embed_low"], 1)
                for t in range(KT):
                    tile = A_TILE[A_PROJ] + t
                    dve.wait_ge(sem["product"], tile + 1)
                    dve.tensor_copy(proj[:, t, :], ps[:, tile % 4, :]).then_inc(sem["drained"], 1)
                    if t == 0:
                        mean_square(dve, mem, sem, 1)
                        root_diagonals(dve, mem, sem, 1)
                        split_low(dve, mem, sem, A_MLP)
                dve.wait_ge(sem["kept"], 2)

                def mlp_first(c0, per, j):
                    for i in range(BC):
                        split_low(dve, mem, sem, c0 + i + 1, per)
                        for t in range(2):
                            tile = A_TILE[c0 + i] + t
                            dve.wait_ge(sem["product"], tile + 1 + per(4 * BC))
                            dve.tensor_tensor(tmp[:, 0, :], ps[:, tile % 4, :], mem.rb[:, :], ALU.mult).then_inc(sem["drained"], 1)
                            dve.wait_ge(sem["drained"], tile + 1 + per(4 * BC))
                            dve.scalar_tensor_tensor(out=tmp[:, 1, :], in0=tmp[:, 0, :], scalar=0.0, in1=tmp[:, 0, :],
                                                     op0=ALU.max, op1=ALU.mult).then_inc(sem["hidden"], 1)
                            dve.wait_ge(sem["hidden_high"], 2 * i + t + 1 + j * KT)
                            dve.tensor_tensor(mem.hl[:, 2 * i + t, :], tmp[:, 1, :], mem.hh[:, 2 * i + t, :].bitcast(F32),
                                              ALU.subtract).then_inc(sem["hidden_low"], 1)

                with dve.Fori(0, FB - 1) as j:
                    def per(n):
                        return j * n

                    mlp_first(A_MLP, per, j)
                    for i in range(BC, 2 * BC):
                        split_low(dve, mem, sem, A_MLP + i + 1, per)
                        for t in range(2):
                            add_to_x(A_TILE[A_MLP + i] + t, 2 * (i - BC) + t, per)
                c0 = A_GATE - 2 * BC
                mlp_first(c0, once, FB - 1)
                for c in range(c0 + BC, A_GATE):
                    split_low(dve, mem, sem, c + 1)
                    for t in range(2):
                        k = 2 * (c - c0 - BC) + t
                        add_to_x(A_TILE[c] + t, k)
                        gain_low(dve, mem, sem, 2, k, gate_gains)
                split_low(dve, mem, sem, A_GATE + 1)
                mean_square(dve, mem, sem, 2)
                root_diagonals(dve, mem, sem, 2)
                dve.wait_ge(sem["kept"], 3)
                for c in range(A_GATE, A_CHUNKS):
                    if c > A_GATE:
                        split_low(dve, mem, sem, c + 1)
                    for t in range(2):
                        n = 2 * (c - A_GATE) + t
                        drain(tmp[:, 0, :], A_TILE[c] + t)
                        dve.wait_ge(sem["gate_out"], n + 1)
                        own.mark(dve.tensor_tensor(tmp[:, 1, :], tmp[:, 1, :], proj[:, n, :], ALU.mult))
                        own.settle()
                        own.mark(dve.tensor_tensor(x[:, n, :], x[:, n, :], tmp[:, 1, :], ALU.add))
                split_low(dve, mem, sem, A_CHUNKS + 1)

            @block.tensor
            def _(pe):
                def gained(n):
                    return lambda k: pe.wait_ge(sem["gain_low"], KT * n + k + 1)

                def linear_chunk(c, high, low, before=None, order=range(KT), after=None, per=once):
                    for t in range(2):
                        tile = A_TILE[c] + t
                        product_tile(pe, mem, sem, c, P * t, tile, high, low, order, before if t == 0 else None, per=per)
                        if after:
                            after(tile)

                first_two_chunks(pe, mem, sem, 0, 0, 0, gained(0))
                linear_chunk(2, mem.gh, mem.gl)
                pe.wait_ge(sem["positioned"], 32)

                def gate_products(tiles):
                    for t in tiles:
                        pe.wait_ge(sem["conv"], t + 1)
                        for g in range(2):
                            if t:
                                pe.wait_ge(sem["gated"], 2 * t - 1 + g)
                            pe.matmul(ps[:, 6 + g, :], gw[:, g, t, :], xc[:, t, :], start=True, stop=True).then_inc(sem["gate_product"], 1)

                gate_products((0,))
                linear_chunk(3, mem.gh, mem.gl, after=lambda tile: gate_products((1,) if tile == A_TILE[3] else (2, 3)))
                for c in range(4, A_V):
                    linear_chunk(c, mem.gh, mem.gl)
                for c in (A_V, A_V + 1):
                    for i in range(QT):
                        token_tile(pe, mem, sem, c, i, A_TILE[c] + i)

                def scores(s):
                    h, i = divmod(s, QT)
                    n, b = P * (i + 1), s % 2
                    if s >= 2:
                        pe.wait_ge(sem["exped"], 2 * (s - 1))
                    for c in range(2):
                        half = slice(DH * c, DH * (c + 1))
                        out = ps[:, 2 * b + c, 0:n]
                        pe.matmul(out, qk[half, h, P * i:n], qk[half, 4 + h, 0:n], start=True, stop=False, skip_group_check=True)
                        last = pe.matmul(out[:, n - P:n], ident, cst[:, C_TRI:C_TRI + P], start=False, stop=True, skip_group_check=True)
                    last.then_inc(sem["scored"], 1)

                def turn(s):
                    h, i = divmod(s, QT)
                    pe.wait_ge(sem["mixed_done"], s + 1)
                    if s:
                        pe.wait_ge(sem["untangled"], s)
                    for k in range(i + 1):
                        last = pe.transpose(ps[:, 5, P * k:P * (k + 1)], mixed[:, s % 2, P * k:P * (k + 1)], ident)
                    last.then_inc(sem["turned"], 1)

                def weigh(h):
                    pe.wait_ge(sem["untangled"], QT * (h + 1))
                    if h:
                        pe.wait_ge(sem["o_squared"], h)
                    for k in range(QT):
                        last = pe.matmul(ps[:, 6, P * k:S], v[:, k, P * h:P * (h + 1)], pt[:, h % 2, k, P * k:S],
                                         start=(k == 0), stop=(k == QT - 1), skip_group_check=True)
                    last.then_inc(sem["weighted"], 1)

                def head_sums(h):
                    pe.wait_ge(sem["o_squared"], h + 1)
                    if h:
                        pe.wait_ge(sem["o_mean"], h)
                    for i in range(QT):
                        last = pe.matmul(ps[:, 4, 8 + i:9 + i], mem.sq[:, h % 2, P * i:P * (i + 1)], ones[:, 0:1],
                                         start=(i == 0), stop=True, skip_group_check=True)
                    last.then_inc(sem["o_summed"], 1)

                def head_spread(h):
                    pe.wait_ge(sem["o_diag"], h + 1)
                    if h:
                        pe.wait_ge(sem["o_ready"], h)
                    pe.matmul(ps[:, 7, :], ones, tmp[:, 3, :], start=True, stop=True).then_inc(sem["o_spread"], 1)

                pe.wait_ge(sem["drained"], A_TILE[A_OUT])
                scores(0)
                scores(1)
                for s in range(STEPS):
                    if s + 2 < STEPS:
                        scores(s + 2)
                    turn(s)
                    h, i = divmod(s, QT)
                    if h and i == 0:
                        weigh(h - 1)
                    if h and i == 1:
                        head_sums(h - 1)
                    if h and i == 3:
                        head_spread(h - 1)
                weigh(HEADS1 - 1)

                def mixer_ready(k):
                    if k == 6:
                        head_sums(HEADS1 - 1)
                    if k == 0:
                        head_spread(HEADS1 - 1)
                    if k >= 4:
                        pe.wait_ge(sem["y_low"], k - 3)
                    else:
                        pe.wait_ge(sem["o_low"], k + 1)

                for c in range(A_OUT, A_PROJ):
                    linear_chunk(c, mem.hh, mem.hl, mixer_ready if c == A_OUT else None, (4, 5, 6, 7, 0, 1, 2, 3))
                pe.wait_ge(sem["embed_low"], 1)
                pe.wait_ge(sem["low"], split_count(A_PROJ))
                for t in range(KT):
                    tile = A_TILE[A_PROJ] + t
                    pe.wait_ge(sem["drained"], tile - 3)
                    for k in range(2):
                        at = D * k + P * t
                        last = three_passes(pe, ps[:, tile % 4, :], mem.wh[:, A_PROJ % 2, at:at + P], mem.wl[:, A_PROJ % 2, at:at + P],
                                            mem.ph[:, k, :], mem.pl[:, k, :], k == 0, k == 1)
                    last.then_inc(sem["product"], 1)
                    if t == 0:
                        sum_squares(pe, mem, sem, 1)
                    if t == 4:
                        spread_root(pe, mem, sem, 1)

                def mlp(c0, per, j, after=None):
                    for i in range(BC):
                        linear_chunk(c0 + i, mem.gh, mem.gl, gained(1) if i == 0 else None, per=per)
                    for i in range(BC, 2 * BC):
                        linear_chunk(c0 + i, mem.hh, mem.hl,
                                     (lambda k: pe.wait_ge(sem["hidden_low"], k + 1 + j * KT)) if i == BC else None, after=after, per=per)

                with pe.Fori(0, FB - 1) as j:
                    mlp(A_MLP, lambda n: j * n, j)
                c0 = A_GATE - 2 * BC
                mlp(c0, once, FB - 1)

                def after_gate(tile):
                    if tile == A_TILE[A_GATE]:
                        sum_squares(pe, mem, sem, 2)
                    if tile == A_TILE[A_GATE] + 1:
                        spread_root(pe, mem, sem, 2)

                for c in range(A_GATE, A_CHUNKS):
                    linear_chunk(c, mem.gh, mem.gl, gained(2) if c == A_GATE else None, after=after_gate)
        clear(nc, used)



B_TILE = {c: 2 * c for c in range(B_V)}
B_TILE.update({B_V: 18, B_V + 1: 22})
B_TILE.update({c: 26 + 2 * (c - B_OUT) for c in range(B_OUT, B_CHUNKS + 1)})

B2_QK, B2_V, B2_CR, B2_U, B2_IQ, B2_IK, B2_SC, B2_MB = 0, 4096, 6144, 7168, 9280, 11328, 11840, 13376
B2_SUM = B2_V
SCORE_BANKS = (0, 1, 4, 5)
SB_IW, SB_TOP = 80, 112


def b_used(c):
    return B_TILE[c - 1]


def second_stack_layer(nc, mem, layer, weights, params, gains, positions):
    ar, ps, cst, par, small, tmp, x = mem.arena, mem.ps, mem.cst, mem.par, mem.small, mem.tmp, mem.x
    qk = ar[:, B2_QK:B2_QK + 4096].rearrange("p (t s) -> p t s", s=S)
    branch = qk
    v = ar[:, B2_V:B2_V + 2048].rearrange("p (t s) -> p t s", s=S)
    cos, sin = ar[:, B2_CR:B2_CR + S], ar[:, B2_CR + S:B2_CR + 2 * S]
    W = PAD + S
    u = ar[:, B2_U:B2_U + 4 * W].rearrange("p (g s) -> p g s", s=W)
    window = [ar[:, B2_SUM + n * W:B2_SUM + (n + 1) * W] for n in range(2)]
    pooled = ar[:, B2_SUM + 2 * W:B2_SUM + 2 * W + S]
    iq = ar[:, B2_IQ:B2_IQ + 2048].rearrange("p (t s) -> p t s", s=S)
    ik = ar[:, B2_IK:B2_IK + S]
    score = ar[:, B2_SC:B2_SC + 3 * S].rearrange("p (i s) -> p i s", s=S)
    mask = ar[:, B2_MB:B2_MB + 1024].bitcast(BF16).rearrange("p (i s) -> p i s", s=S)
    prob = tmp
    scaled = ar[:, B2_IK + 1024:B2_IK + 2048].rearrange("p (b s) -> p b s", b=2)
    pt = [ar[:, a:a + 2048].rearrange("p (k s) -> p k s", s=S) for a in (B2_IQ, B2_U)]
    weight_rows = small[:, SB_IW:SB_IW + 32].rearrange("p (i h) -> p i h", h=HEADS2)
    top = small[:, SB_TOP:SB_TOP + 24].rearrange("p (i e) -> p i e", e=8)
    wpool = par[:, BP_WPOOL:BP_WPOOL + 4 * P].rearrange("p (g n) -> p g n", g=4)
    ident = cst[:, C_ID:C_ID + P]
    STEPS = QT * HEADS2
    B_START = DEPTH * A_CHUNKS
    pre_ff = par[:, BP_FPRE:BP_FPRE + KT]
    LOGITS = [(i, h) for i in range(1, QT) for h in range(HEADS2)]

    with ExitStack() as ctx:
        sem, used = semaphores(nc, ctx, (
            "loaded0 loaded1 next_gains vectors positioned high low product drained squared gathered summed mean root diag spread kept gain_high "
            "gain_low own tables turned_tables weights_turned masked swapped rotated logit rectified weighed windowed pooled_ready pool_product pool_high pool_low "
            "scored maxed exped scaled_done turned untangled weighted pair_high pair_low updated branch_scaled added zeroed hidden hidden_high "
            "hidden_low padded pool_own"))
        with nc.Block() as block:

            @block.sync
            def _(sp):
                def chunk(c, per=once, j=None):
                    row = (layer * B_CHUNKS + (B_START + c)) * P
                    if j is not None:
                        row = (layer * B_CHUNKS + j * (2 * BC) + (B_START + c)) * P
                    load_chunk(sp, mem, sem, weights, row, c, per)

                rows = sp.snap(layer * P)
                sp.dma_start(par[:, 0:BP_N], params[bass.ds(rows, P), :]).then_inc(sem["vectors"], 16)
                sp.dma_start(tmp[:, 0, :].bitcast(I32), positions).then_inc(sem["positioned"], 16)
                for c in range(2, B_FF):
                    chunk(c)
                with sp.Fori(0, FB) as j:
                    for i in range(2 * BC):
                        chunk(B_FF + i, lambda n: j * n, j)
                load_next(sp, mem, sem, weights, gains, (layer * B_CHUNKS + (B_START + B_CHUNKS)) * P, (layer + (DEPTH + 1)) * P, B_CHUNKS)

            @block.gpsimd
            def _(pool):
                own = Steps(pool, sem["pool_own"])
                pool.memset(u[:, :, 0:PAD], 0.0).then_inc(sem["padded"], 1)
                gather_squares(pool, mem, sem, 0)
                one_over_root(pool, mem, sem, 0)
                pool.wait_ge(sem["low"], split_count(3))
                split_low(pool, mem, sem, 4)
                split_low(pool, mem, sem, 5)

                def add_swapped(n):
                    pool.wait_ge(sem["swapped"], n + 1)
                    pool.wait_ge(sem["drained"], B_TILE[B_Q] + n + 1)
                    pool.tensor_tensor(qk[:, n, :], qk[:, n, :], tmp[:, 2 + n % 2, :], ALU.add).then_inc(sem["rotated"], 1)

                for g in range(4):
                    pool.wait_ge(sem["drained"], B_TILE[B_U] + g + 1)
                    pool.wait_ge(sem["padded"], 1)
                    if g:
                        pool.wait_ge(sem["pooled_ready"], g)
                    source, reach = u[:, g, :], 1
                    for n in range(g + 1):
                        own.settle() if own.count else None
                        last = pool.tensor_tensor(window[n % 2][:, 2 * reach - 1:W], source[:, 2 * reach - 1:W],
                                                  source[:, reach - 1:W - reach], ALU.add)
                        if n < g:
                            own.mark(last)
                        source, reach = window[n % 2], 2 * reach
                    last.then_inc(sem["windowed"], 1)
                    if g == 0:
                        split_low(pool, mem, sem, 6)
                    add_swapped(2 * g)
                    split_low(pool, mem, sem, 7 + g)
                    add_swapped(2 * g + 1)
                split_low(pool, mem, sem, B_OUT)
                split_low(pool, mem, sem, B_OUT + 1)
                for n in (1, 2):
                    gather_squares(pool, mem, sem, n)
                    one_over_root(pool, mem, sem, n)
                pool.wait_ge(sem["updated"], KT)
                pool.memset(branch[:, :, :], 0.0).then_inc(sem["zeroed"], 1)
                gather_squares(pool, mem, sem, 3)
                one_over_root(pool, mem, sem, 3)
                for n in range(KT // 2):
                    k = 2 * n + 1
                    pool.wait_ge(sem["branch_scaled"], n + 1)
                    pool.tensor_tensor(x[:, k, :], x[:, k, :], tmp[:, k % 4, :], ALU.add).then_inc(sem["added"], 1)

            @block.scalar
            def _(act):
                for k in range(KT):
                    gain_high(act, mem, sem, k, mem.first_gains)
                    square_slice(act, mem, sem, 0, k, x)
                act.wait_ge(sem["tables"], 1)
                act.activation(sin, tmp[:, 1, :], ACT.Sin, scale=cst[:, C_SIGN:C_SIGN + 1]).then_inc(sem["turned_tables"], 1)
                act.activation(cos, tmp[:, 0, :], ACT.Sin, scale=-1.0, bias=cst[:, C_HPI:C_HPI + 1]).then_inc(sem["turned_tables"], 1)
                split_high(act, mem, sem, 2, b_used(2))
                keep_root(act, mem, sem, 0)
                for c in (3, 4):
                    split_high(act, mem, sem, c, b_used(c))
                for s, (i, h) in enumerate(LOGITS):
                    n = P * (i + 1)
                    act.wait_ge(sem["logit"], s + 1)
                    if s >= 2:
                        act.wait_ge(sem["weighed"], s - 1)
                    act.activation(tmp[:, s % 2, 0:n], ps[:, 6 + s % 2, 0:n], ACT.Relu, scale=DH ** -0.5).then_inc(sem["rectified"], 1)
                    if s == 1:
                        split_high(act, mem, sem, 5, b_used(5))
                split_high(act, mem, sem, 6, b_used(6))
                act.wait_ge(sem["vectors"], 16)
                for g in range(4):
                    split_high(act, mem, sem, 7 + g, b_used(7 + g))
                    act.wait_ge(sem["pool_product"], g + 1)
                    act.activation(mem.hh[:, g, :], ps[:, 6 + g % 2, :], ACT.Copy,
                                   scale=par[:, BP_SCALE + g:BP_SCALE + g + 1]).then_inc(sem["pool_high"], 1)
                act.wait_ge(sem["drained"], B_TILE[B_V])
                for i in range(2 * QT):
                    tile, c = B_TILE[B_V] + i, i // QT
                    if i == QT:
                        split_high(act, mem, sem, B_OUT, b_used(B_OUT))
                    act.wait_ge(sem["product"], tile + 1)
                    act.activation(v[:, i % QT, c * CW:(c + 1) * CW], ps[:, tile % 4, 0:CW], ACT.Copy,
                                   scale=small[:, QT + i % QT:QT + i % QT + 1]).then_inc(sem["drained"], 1)

                def exponents(s):
                    n, b = P * (s % QT + 1), s % 4
                    act.wait_ge(sem["maxed"], s + 1)
                    if s >= 4:
                        act.wait_ge(sem["scaled_done"], s - 3)
                    act.activation(prob[:, b, 0:n], ps[:, SCORE_BANKS[b], 0:n], ACT.Exp, scale=DH ** -0.5, bias=small[:, SM_NEG + b:SM_NEG + b + 1],
                                   accum_out=small[:, SM_SUM + b:SM_SUM + b + 1]).then_inc(sem["exped"], 1)

                def untangle(s):
                    h, i = divmod(s, QT)
                    act.wait_ge(sem["turned"], s + 1)
                    if h >= 2:
                        act.wait_ge(sem["weighted"], h - 1)
                    act.activation(pt[h % 2][:, 0:i + 1, P * i:P * (i + 1)],
                                   ps[:, 2 + s % 2, 0:P * (i + 1)].rearrange("p (k q) -> p k q", q=P), ACT.Copy).then_inc(sem["untangled"], 1)

                def pair_high(j):
                    act.wait_ge(sem["weighted"], 2 * j + 2)
                    act.activation(mem.hh[:, 4 + j, :], ps[:, 6 + j % 2, :], ACT.Copy).then_inc(sem["pair_high"], 1)

                exponents(0)
                for s in range(STEPS):
                    if s + 1 < STEPS:
                        exponents(s + 1)
                    untangle(s)
                    if s >= 8 and s % 8 == 2:
                        pair_high(s // 8 - 1)
                    if s == 4:
                        split_high(act, mem, sem, B_OUT + 1, b_used(B_OUT + 1))
                pair_high(3)
                for c in range(B_OUT, B_FF):
                    if B_OUT + 2 <= c + 1:
                        split_high(act, mem, sem, c + 1, b_used(c + 1))
                    for t in range(2):
                        act.wait_ge(sem["drained"], B_TILE[c] + t + 1)
                        square_slice(act, mem, sem, 1, 2 * (c - B_OUT) + t, branch)
                split_high(act, mem, sem, B_FF + 1, b_used(B_FF + 1))
                keep_root(act, mem, sem, 1)
                for k in range(KT):
                    act.wait_ge(sem["updated"], k + 1)
                    gain_high(act, mem, sem, k, pre_ff)
                    square_slice(act, mem, sem, 2, k, x)
                keep_root(act, mem, sem, 2)

                def mlp_first(c0, per, j):
                    for i in range(BC):
                        if i == 0:
                            split_high(act, mem, sem, c0 + 2, b_used(c0 + 2), per)
                        for t in range(2):
                            act.wait_ge(sem["hidden"], 2 * i + t + 1 + j * KT)
                            act.activation(mem.hh[:, 2 * i + t, :], tmp[:, 1, :], ACT.Copy).then_inc(sem["hidden_high"], 1)
                        if i:
                            split_high(act, mem, sem, c0 + i + 2, b_used(c0 + i + 2), per)

                with act.Fori(0, FB - 1) as j:
                    def per(n):
                        return j * n

                    mlp_first(B_FF, per, j)
                    for i in range(BC, 2 * BC):
                        split_high(act, mem, sem, B_FF + i + 2, b_used(B_FF + i + 2), per)
                c0 = B_CHUNKS - 2 * BC
                mlp_first(c0, once, FB - 1)
                for c in range(c0 + BC, B_CHUNKS):
                    for t in range(2):
                        act.wait_ge(sem["drained"], B_TILE[c] + t + 1)
                        square_slice(act, mem, sem, 3, 2 * (c - c0 - BC) + t, branch)
                    split_high(act, mem, sem, c + 2, b_used(c + 2))
                keep_root(act, mem, sem, 3)

            @block.vector
            def _(dve):
                own = Steps(dve, sem['own'])
                for k in range(KT):
                    gain_low(dve, mem, sem, 0, k, mem.first_gains)
                dve.wait_ge(sem["positioned"], 16)
                rotary_angles(dve, own, mem, tmp[:, 0, :], tmp[:, 1, :]).then_inc(sem["tables"], 1)
                own.mark(dve.tensor_copy(mask[:, 0, 0:P], cst[:, C_CHUNK:C_CHUNK + P]))
                mean_square(dve, mem, sem, 0)
                root_diagonals(dve, mem, sem, 0)
                split_low(dve, mem, sem, 2)
                dve.wait_ge(sem["kept"], 1)
                dve.wait_ge(sem["turned_tables"], 2)
                own.mark(dve.tensor_tensor(sin, sin, mem.rb[:, :], ALU.mult))
                own.mark(dve.tensor_tensor(cos, cos, mem.rb[:, :], ALU.mult))
                own.settle()
                for t in range(4):
                    rotate(dve, own, mem, sem, t, iq[:, t, :], cos, sin)
                    if t == 1:
                        split_low(dve, mem, sem, 3)
                rotate(dve, own, mem, sem, 4, ik, cos, sin)
                dve.wait_ge(sem["product"], 6)
                dve.wait_ge(sem["spread"], 1)
                own.settle()
                dve.tensor_tensor(tmp[0:HEADS2, 3, :], ps[0:HEADS2, 5 % 4, :], mem.rb[0:HEADS2, :], ALU.mult)\
                    .then_inc(sem["drained"], 1)

                def drain_u(tile):
                    dve.wait_ge(sem["product"], tile + 1)
                    dve.tensor_tensor(u[:, tile - B_TILE[B_U], PAD:W], ps[:, tile % 4, :], mem.rb[:, :], ALU.mult)\
                        .then_inc(sem["drained"], 1)

                dve.wait_ge(sem["padded"], 1)
                drain_u(6)
                drain_u(7)
                dve.wait_ge(sem["weights_turned"], 1)
                own.mark(dve.tensor_scalar(small[:, SB_IW:SB_IW + QT * HEADS2], ps[:, 5, 0:QT * HEADS2], HEADS2 ** -0.5, None, ALU.mult))
                own.settle()
                for s, (i, h) in enumerate(LOGITS):
                    n = P * (i + 1)
                    dve.wait_ge(sem["rectified"], s + 1)
                    out, scale = score[:, i - 1, 0:n], weight_rows[:, i, h:h + 1]
                    if h == 0:
                        dve.tensor_scalar(out, tmp[:, s % 2, 0:n], scale, None, ALU.mult).then_inc(sem["weighed"], 1)
                    else:
                        dve.wait_ge(sem["weighed"], s)
                        dve.scalar_tensor_tensor(out=out, in0=tmp[:, s % 2, 0:n], scalar=scale, in1=out,
                                                 op0=ALU.mult, op1=ALU.add).then_inc(sem["weighed"], 1)
                dve.wait_ge(sem["weighed"], len(LOGITS))
                for i in range(1, QT):
                    edge = score[:, i - 1, P * i:P * (i + 1)]
                    own.mark(dve.tensor_tensor(edge, edge, cst[:, C_CHUNK:C_CHUNK + P], ALU.add))

                def pick():
                    own.settle()
                    for i in range(1, QT):
                        own.mark(dve.max(top[:, i - 1, :], score[:, i - 1, 0:P * (i + 1)]))
                    found = own.count
                    for i in range(1, QT):
                        values = score[:, i - 1, 0:P * (i + 1)]
                        dve.wait_ge(sem["own"], found - (QT - 1 - i))
                        own.mark(dve.match_replace(out=values, in_to_replace=top[:, i - 1, :], in_values=values, imm_value=MARK))

                rounds = [0]

                def picks(n):
                    for _ in range(n):
                        pick()
                        rounds[0] += 1

                drain_u(8)
                picks(1)
                drain_u(9)
                picks(3)

                def pool_values(g):
                    w = WINDOWS[g]
                    total = window[g % 2][:, PAD:W]
                    dve.wait_ge(sem["windowed"], g + 1)
                    if g:
                        dve.wait_ge(sem["pool_product"], g)
                    own.settle()
                    own.mark(dve.scalar_tensor_tensor(out=pooled, in0=total, scalar=1.0 / w, in1=u[:, g, PAD:W],
                                                      op0=ALU.mult, op1=ALU.subtract))
                    own.settle()
                    own.mark(dve.tensor_tensor(pooled[:, 0:PAD], total[:, 0:PAD], cst[:, C_CNT + PAD * g:C_CNT + PAD * (g + 1)], ALU.mult))
                    own.settle()
                    dve.tensor_tensor(pooled[:, 0:PAD], pooled[:, 0:PAD], u[:, g, PAD:2 * PAD], ALU.subtract).then_inc(sem["pooled_ready"], 1)

                dve.wait_ge(sem["vectors"], 16)

                def pool_low(g):
                    dve.wait_ge(sem["pool_high"], g + 1)
                    dve.scalar_tensor_tensor(out=mem.hl[:, g, :], in0=ps[:, 6 + g % 2, :], scalar=par[:, BP_SCALE + g:BP_SCALE + g + 1],
                                             in1=mem.hh[:, g, :].bitcast(F32), op0=ALU.mult, op1=ALU.subtract).then_inc(sem["pool_low"], 1)

                def rotate_first(tile, n):
                    swapped = tmp[:, 2 + n % 2, :]
                    dve.wait_ge(sem["product"], tile + 1)
                    if n >= 2:
                        dve.wait_ge(sem["rotated"], n - 1)
                    own.settle()
                    own.mark(dve.stream_shuffle(swapped, ps[:, tile % 4, :], SWAP))
                    dve.tensor_tensor(qk[:, n, :], ps[:, tile % 4, :], cos, ALU.mult).then_inc(sem["drained"], 1)
                    own.settle()
                    dve.tensor_tensor(swapped, swapped, sin, ALU.mult).then_inc(sem["swapped"], 1)

                for c in range(B_Q, B_V):
                    for t in range(2):
                        rotate_first(B_TILE[c] + t, 2 * (c - B_Q) + t)
                        if t == 0:
                            pool_values(c - B_Q)
                        elif c > B_Q:
                            pool_low(c - B_Q - 1)
                        picks(1)
                picks(2)
                pool_low(3)
                picks(TOPK // 8 - rounds[0])
                own.settle()
                for i in range(1, QT):
                    n = P * (i + 1)
                    dve.tensor_scalar(mask[:, i, 0:n], score[:, i - 1, 0:n], 0.9 * MARK, NEG, ALU.is_gt, ALU.mult)\
                        .then_inc(sem["masked"], 1)

                def maxima(s):
                    n, b = P * (s % QT + 1), s % 4
                    dve.wait_ge(sem["scored"], s + 1)
                    own.mark(dve.tensor_reduce(small[:, SM_MAX + b:SM_MAX + b + 1], ps[:, SCORE_BANKS[b], 0:n], AX.X, ALU.max))
                    own.settle()
                    dve.tensor_scalar(small[:, SM_NEG + b:SM_NEG + b + 1], small[:, SM_MAX + b:SM_MAX + b + 1],
                                      -(DH ** -0.5), None, ALU.mult).then_inc(sem["maxed"], 1)

                def scale_rows(s):
                    n, b = P * (s % QT + 1), s % 4
                    inv = small[:, SM_INV + b:SM_INV + b + 1]
                    dve.wait_ge(sem["exped"], s + 1)
                    own.mark(dve.reciprocal(inv, small[:, SM_SUM + b:SM_SUM + b + 1]))
                    own.settle()
                    if s >= 2:
                        dve.wait_ge(sem["turned"], s - 1)
                    dve.tensor_scalar(scaled[:, s % 2, 0:n], prob[:, b, 0:n], inv, None, ALU.mult).then_inc(sem["scaled_done"], 1)

                def pair_low(j):
                    dve.wait_ge(sem["pair_high"], j + 1)
                    dve.tensor_tensor(mem.hl[:, 4 + j, :], ps[:, 6 + j % 2, :], mem.hh[:, 4 + j, :].bitcast(F32),
                                      ALU.subtract).then_inc(sem["pair_low"], 1)

                maxima(0)
                maxima(1)
                for s in range(STEPS):
                    scale_rows(s)
                    if s + 2 < STEPS:
                        maxima(s + 2)
                    if s >= 8 and s % 8 == 3:
                        pair_low(s // 8 - 1)
                pair_low(3)
                dve.wait_ge(sem["low"], split_count(B_OUT + 1))
                for c in range(B_OUT, B_FF):
                    if B_OUT + 2 <= c + 1:
                        split_low(dve, mem, sem, c + 1)
                    for t in range(2):
                        tile = B_TILE[c] + t
                        dve.wait_ge(sem["product"], tile + 1)
                        dve.tensor_copy(branch[:, 2 * (c - B_OUT) + t, :], ps[:, tile % 4, :]).then_inc(sem["drained"], 1)
                mean_square(dve, mem, sem, 1)
                root_diagonals(dve, mem, sem, 1)
                split_low(dve, mem, sem, B_FF + 1)

                def scaled_branch(k, gains, place):
                    return dve.scalar_tensor_tensor(out=tmp[:, place, :], in0=branch[:, k, :], scalar=par[:, gains + k:gains + k + 1],
                                                    in1=mem.rb[:, :], op0=ALU.mult, op1=ALU.mult)

                dve.wait_ge(sem["kept"], 2)
                own.settle()
                own.mark(scaled_branch(0, BP_GPOST, 0))
                for k in range(KT):
                    if k + 1 < KT:
                        if k:
                            dve.wait_ge(sem["updated"], k)
                        own.mark(scaled_branch(k + 1, BP_GPOST, (k + 1) % 2))
                    dve.wait_ge(sem["own"], own.count - (k + 1 < KT))
                    dve.tensor_tensor(x[:, k, :], x[:, k, :], tmp[:, k % 2, :], ALU.add).then_inc(sem["updated"], 1)
                    if k:
                        gain_low(dve, mem, sem, 1, k - 1, pre_ff)
                gain_low(dve, mem, sem, 1, KT - 1, pre_ff)
                mean_square(dve, mem, sem, 2)
                root_diagonals(dve, mem, sem, 2)
                def mlp_first(c0, per, j):
                    for i in range(BC):
                        if i == 0:
                            split_low(dve, mem, sem, c0 + 2, per)
                            dve.wait_ge(sem["kept"], 3)
                        for t in range(2):
                            tile = B_TILE[c0 + i] + t
                            dve.wait_ge(sem["product"], tile + 1 + per(4 * BC))
                            dve.tensor_tensor(tmp[:, 0, :], ps[:, tile % 4, :], mem.rb[:, :], ALU.mult).then_inc(sem["drained"], 1)
                            dve.wait_ge(sem["drained"], tile + 1 + per(4 * BC))
                            dve.scalar_tensor_tensor(out=tmp[:, 1, :], in0=tmp[:, 0, :], scalar=0.0, in1=tmp[:, 0, :],
                                                     op0=ALU.max, op1=ALU.mult).then_inc(sem["hidden"], 1)
                            dve.wait_ge(sem["hidden_high"], 2 * i + t + 1 + j * KT)
                            dve.tensor_tensor(mem.hl[:, 2 * i + t, :], tmp[:, 1, :], mem.hh[:, 2 * i + t, :].bitcast(F32),
                                              ALU.subtract).then_inc(sem["hidden_low"], 1)
                        if i:
                            split_low(dve, mem, sem, c0 + i + 2, per)

                def mlp_second(c0, per):
                    dve.wait_ge(sem["zeroed"], 1)
                    for i in range(BC, 2 * BC):
                        for t in range(2):
                            tile, k = B_TILE[c0 + i] + t, 2 * (i - BC) + t
                            dve.wait_ge(sem["product"], tile + 1 + per(4 * BC))
                            dve.tensor_tensor(branch[:, k, :], branch[:, k, :], ps[:, tile % 4, :], ALU.add).then_inc(sem["drained"], 1)
                        if c0 + i + 2 <= B_CHUNKS:
                            split_low(dve, mem, sem, c0 + i + 2, per)

                with dve.Fori(0, FB - 1) as j:
                    def per(n):
                        return j * n

                    mlp_first(B_FF, per, j)
                    mlp_second(B_FF, per)
                mlp_first(B_CHUNKS - 2 * BC, once, FB - 1)
                mlp_second(B_CHUNKS - 2 * BC, once)
                mean_square(dve, mem, sem, 3)
                root_diagonals(dve, mem, sem, 3)
                split_low(dve, mem, sem, B_CHUNKS + 1)
                dve.wait_ge(sem["kept"], 4)
                for k in range(0, KT, 2):
                    own.settle()
                    if k >= 4:
                        dve.wait_ge(sem["added"], k // 2 - 1)
                    own.mark(scaled_branch(k, BP_FPOST, k % 4))
                    scaled_branch(k + 1, BP_FPOST, k % 4 + 1).then_inc(sem["branch_scaled"], 1)
                    own.settle()
                    own.mark(dve.tensor_tensor(x[:, k, :], x[:, k, :], tmp[:, k % 4, :], ALU.add))

            @block.tensor
            def _(pe):
                def gained(n):
                    return lambda k: pe.wait_ge(sem["gain_low"], KT * n + k + 1)

                def linear_chunk(c, high, low, before=None, order=range(KT), after=None, per=once):
                    for t in range(2):
                        tile = B_TILE[c] + t
                        product_tile(pe, mem, sem, c, P * t, tile, high, low, order, before if t == 0 else None, per=per)
                        if after:
                            after(tile)

                first_two_chunks(pe, mem, sem, 0, 0, 0, gained(0))
                product_tile(pe, mem, sem, B_IKW, 0, 4, mem.gh, mem.gl)
                product_tile(pe, mem, sem, B_IKW, P, 5, mem.gh, mem.gl, width=HEADS2)
                linear_chunk(3, mem.gh, mem.gl)
                pe.wait_ge(sem["drained"], 6)
                for i in range(QT):
                    last = pe.transpose(ps[:, 5, HEADS2 * i:HEADS2 * (i + 1)], tmp[0:HEADS2, 3, P * i:P * (i + 1)], ident[0:HEADS2, 0:HEADS2])
                last.then_inc(sem["weights_turned"], 1)

                def logit(s):
                    i, h = LOGITS[s]
                    half = slice(DH * (h % 2), DH * (h % 2 + 1))
                    if s >= 2:
                        pe.wait_ge(sem["rectified"], s - 1)
                    pe.matmul(ps[:, 6 + s % 2, 0:P * (i + 1)], iq[half, h // 2, P * i:P * (i + 1)], ik[half, 0:P * (i + 1)],
                              start=True, stop=True).then_inc(sem["logit"], 1)

                def three_logits(k):
                    for s in range(3 * k, 3 * k + 3):
                        logit(s)

                product_tile(pe, mem, sem, 4, 0, B_TILE[4], mem.gh, mem.gl, before=three_logits)
                product_tile(pe, mem, sem, 4, P, B_TILE[4] + 1, mem.gh, mem.gl)
                linear_chunk(5, mem.gh, mem.gl)

                pe.wait_ge(sem["vectors"], 16)

                def pool_product(g):
                    pe.wait_ge(sem["pooled_ready"], g + 1)
                    pe.wait_ge(sem["rectified"], len(LOGITS))
                    if g >= 2:
                        pe.wait_ge(sem["pool_low"], g - 1)
                    pe.matmul(ps[:, 6 + g % 2, :], wpool[:, g, :], pooled, start=True, stop=True).then_inc(sem["pool_product"], 1)

                for c in (6, 7, 8):
                    linear_chunk(c, mem.gh, mem.gl, after=lambda tile: pool_product(c - 6) if tile == B_TILE[c] else None)
                for c in (B_V, B_V + 1):
                    for i in range(QT):
                        token_tile(pe, mem, sem, c, i, B_TILE[c] + i)
                        if c == B_V and i == 1:
                            pool_product(3)

                def scores(s):
                    h, i = divmod(s, QT)
                    n = P * (i + 1)
                    half = slice(DH * (h % 2), DH * (h % 2 + 1))
                    bank = SCORE_BANKS[s % 4]
                    if s >= 4:
                        pe.wait_ge(sem["exped"], s - 3)
                    pe.matmul(ps[:, bank, 0:n], qk[half, h // 2, P * i:n], qk[half, 4 + h // 2, 0:n],
                              start=True, stop=False, skip_group_check=True)
                    pe.matmul(ps[:, bank, 0:n], mem.idb[:, :], mask[:, i, 0:n], start=False, stop=True,
                              skip_group_check=True).then_inc(sem["scored"], 1)

                def turn(s):
                    h, i = divmod(s, QT)
                    pe.wait_ge(sem["scaled_done"], s + 1)
                    if s >= 2:
                        pe.wait_ge(sem["untangled"], s - 1)
                    for k in range(i + 1):
                        last = pe.transpose(ps[:, 2 + s % 2, P * k:P * (k + 1)], scaled[:, s % 2, P * k:P * (k + 1)], ident)
                    last.then_inc(sem["turned"], 1)

                def weigh(h):
                    j = h // 2
                    pe.wait_ge(sem["untangled"], QT * (h + 1))
                    if h % 2 == 0 and j >= 2:
                        pe.wait_ge(sem["pair_low"], j - 1)
                    out = ps[DH * (h % 2):DH * (h % 2 + 1), 6 + j % 2, :]
                    for k in range(QT):
                        last = pe.matmul(out[:, P * k:S], v[:, k, DH * h:DH * (h + 1)], pt[h % 2][:, k, P * k:S],
                                         start=(k == 0), stop=(k == QT - 1), skip_group_check=True)
                    last.then_inc(sem["weighted"], 1)

                pe.wait_ge(sem["drained"], B_TILE[B_OUT])
                pe.wait_ge(sem["masked"], QT - 1)
                pe.wait_ge(sem["rotated"], 8)
                for s in range(3):
                    scores(s)
                for s in range(STEPS):
                    if s + 3 < STEPS:
                        scores(s + 3)
                    turn(s)
                    if s >= QT and s % QT == 1:
                        weigh(s // QT - 1)
                weigh(HEADS2 - 1)

                def mixer_ready(k):
                    if k < 4:
                        pe.wait_ge(sem["pool_low"], k + 1)
                    else:
                        pe.wait_ge(sem["pair_low"], k - 3)

                for c in range(B_OUT, B_FF):
                    linear_chunk(c, mem.hh, mem.hl, mixer_ready if c == B_OUT else None)
                sum_squares(pe, mem, sem, 1)
                spread_root(pe, mem, sem, 1)

                def mlp_second(c0, per, j):
                    for i in range(BC, 2 * BC):
                        linear_chunk(c0 + i, mem.hh, mem.hl,
                                     (lambda k: pe.wait_ge(sem["hidden_low"], k + 1 + j * KT)) if i == BC else None, per=per)

                def mlp_first(c0, per, chunks):
                    for i in chunks:
                        linear_chunk(c0 + i, mem.gh, mem.gl, per=per)

                pe.wait_ge(sem["drained"], B_TILE[B_FF])
                first_two_chunks(pe, mem, sem, B_FF, B_TILE[B_FF], 2, gained(1))
                mlp_first(B_FF, once, range(2, BC))
                mlp_second(B_FF, once, 0)
                with pe.Fori(1, FB) as j:
                    def per(n):
                        return j * n

                    mlp_first(B_FF, per, range(BC))
                    mlp_second(B_FF, per, j)
                sum_squares(pe, mem, sem, 3)
                spread_root(pe, mem, sem, 3)
        clear(nc, used)



def chunks(w):
    k, n = w.shape
    return w.reshape(k // P, P, n // CW, CW).transpose(2, 1, 0, 3).reshape(-1, k // P * CW)


def columns(v):
    return v.reshape(-1, P).T


def constant_table():
    t = np.zeros((P, C_N), np.float32)
    p = np.arange(P)
    t[:, C_ID:C_ID + P] = np.eye(P)
    t[:, C_ONES:C_ONES + P] = 1.0
    t[:, C_TRI:C_TRI + P] = np.where(p[:, None] >= p[None, :], 0.0, NEG)
    t[:, C_CHUNK:C_CHUNK + P] = np.where(p[:, None] // 64 >= p[None, :] // 64, 0.0, NEG)
    d = p % DH
    freq = np.float32(THETA) ** (-np.arange(ROT_HALF, dtype=np.float32) / ROT_HALF)
    t[:, C_FREQ] = np.where(d < 2 * ROT_HALF, freq[d % ROT_HALF], 0.0)
    t[:, C_SIGN] = np.where(d < ROT_HALF, -1.0, 1.0)
    for g, w in enumerate(WINDOWS):
        t[:, C_CNT + PAD * g:C_CNT + PAD * (g + 1)] = 1.0 / np.minimum(np.arange(PAD) + 1, w)
    t[:, C_HPI] = np.pi / 2
    t[:, C_MHALF:C_MHALF + QT] = -0.5
    return t


def launch_arrays(inp):
    f = {k: np.asarray(a) for k, a in inp.items()}
    wa, pa, gates, embed = [], [], [], []
    for l in range(DEPTH):
        w = f["w_in"][l]
        q, k, v, xr, gr = (w[:, a:b] for a, b in ((0, 512), (512, 1024), (1024, 1536), (1536, 2048), (2048, 2560)))
        wa += [chunks(m) for m in (xr, gr, q, k, v, f["w_out"][l])]
        wa += [f["w_ple_proj"][l].reshape(2, P, D).transpose(1, 0, 2).reshape(P, CHUNK)]
        for j in range(FB):
            wa += [chunks(f["w_mlp_in"][l][:, D * j:D * (j + 1)]), chunks(f["w_mlp_out"][l][D * j:D * (j + 1)])]
        wa += [chunks(f["w_ple_gate"][l])]
        wide = lambda a: np.broadcast_to(a.reshape(1, -1), (P, a.size))
        lam_init = 0.8 - 0.6 * math.exp(-0.3 * l)
        pa += [np.concatenate([
            columns(f["g_mix"][l]), columns(f["g_mlp"][l]), columns(f["g_ple"][l]), columns(f["g_subln"][l]),
            *[columns(f["conv_w"][l][t]) for t in range(CONV)], columns(f["conv_b"][l]),
            columns(f["b_gate_a"][l]), columns(f["b_gate_x"][l]), columns(f["lru_lambda"][l]),
            wide(f["lam_q"][l]), wide(f["lam_k"][l]),
            np.full((P, 1), lam_init, np.float32), np.full((P, 1), 1.0 - lam_init, np.float32)], axis=1)]
        g = np.zeros((2, 4, P, P), np.float32)
        for n, name in enumerate(("w_gate_a", "w_gate_x")):
            g[n, :, :64, :64] = f[name][l][0::2]
            g[n, :, 64:, 64:] = f[name][l][1::2]
        gates += [g.transpose(2, 0, 1, 3).reshape(P, -1)]
        embed += [f["p"][l, 0].T.reshape(2, P, S).transpose(1, 0, 2).reshape(P, -1)]
    wb, pb = [], []
    for l in range(DEPTH):
        w = f["w_in_2"][l]
        u, q, k, v, iq, ik, iw = np.split(w, np.cumsum((512, 512, 512, 512, 512, 64)), axis=1)
        ikw = np.zeros((D, CW), np.float32)
        ikw[:, 0:64], ikw[:, 64:128], ikw[:, 128:136] = ik, ik, iw
        wb += [chunks(m) for m in (iq, ikw, u, q, k, v, f["w_out_2"][l])]
        for j in range(FB):
            wb += [chunks(f["w_ff1_2"][l][:, D * j:D * (j + 1)]), chunks(f["w_ff2_2"][l][D * j:D * (j + 1)])]
        pb += [np.concatenate([
            columns(f["g_pre_mix_2"][l]), columns(f["g_post_mix_2"][l]), columns(f["g_pre_ffn_2"][l]),
            columns(f["g_post_ffn_2"][l]), columns(f["pool_scale_2"][l]),
            f["w_pool_2"][l].transpose(1, 0, 2).reshape(P, -1)], axis=1)]
    table = constant_table()
    table[:, C_GFIN:C_GFIN + KT] = columns(f["g_final"])
    spread = lambda a: np.broadcast_to(a.reshape(1, S), (P, S))
    wb += [np.zeros((2 * P, CHUNK), np.float32)]
    first = [columns(g) for name in ("g_mix", "g_pre_mix_2") for g in f[name][:DEPTH]] + [np.zeros((P, KT), np.float32)]
    out = {
        "weights": np.concatenate(wa + wb), "params_a": np.concatenate(pa),
        "params_b": np.concatenate(pb), "gains": np.concatenate(first), "gates": np.concatenate(gates), "embed": np.concatenate(embed),
        "constants": table, "positions": np.concatenate([spread(f["positions"]), spread(f["positions_2"])]),
        "xt": f["x"][0].T,
    }
    return {n: np.ascontiguousarray(a) for n, a in out.items()}


def kernel(**inputs):
    import concourse.bacc as bacc
    from concourse.bass_utils import run_bass_kernel_spmd

    nc = bacc.Bacc("TRN2", target_bir_lowering=False, num_devices=1)
    arrays = {f"in_{name}": a for name, a in launch_arrays(inputs).items()}
    args = [nc.dram_tensor(name, a.shape, mybir.dt.from_np(a.dtype), kind="ExternalInput").ap() for name, a in arrays.items()]
    args.append(nc.dram_tensor("out_yt", (D, S), F32, kind="ExternalOutput").ap())
    build(nc, *args)
    r = run_bass_kernel_spmd(nc, [arrays], core_ids=[0])
    return np.ascontiguousarray(r.results[0]["out_yt"].T).reshape(1, S, D)
```
